# Optimizing a Trainium2 kernel written in Bass

```python
import math
import jax, jax.numpy as jnp
from jax import lax
import numpy as np

D_MODEL = 1024
BATCH = 1
SEQ = 1024
DEPTH = 1

CHUNK = 64
MEM_LEN = 256
W_A = D_MODEL
CONV_A = 3
W_B = D_MODEL
CONV_B = 31
W_X = D_MODEL
N_HEADS_X = 4
HEAD_DIM_X = W_X // N_HEADS_X
EPS = 1e-6

SPLIT_SIZES = (
    W_A, W_A, W_A, W_A,
    W_B, W_B, W_B,
    W_X, W_X,
    D_MODEL, D_MODEL, D_MODEL,
)
IN_COLS = sum(SPLIT_SIZES)
SPLIT_POINTS = tuple(int(v) for v in np.cumsum(SPLIT_SIZES)[:-1])

kernel_name = "hybrid_shortconv_conformer_memxattn_gated"

def rmsnorm(x, g):
    xf = x.astype(jnp.float32)
    y = xf * lax.rsqrt(jnp.mean(xf * xf, axis=-1, keepdims=True) + EPS)
    return (y * g.astype(jnp.float32)).astype(x.dtype)

def layernorm(x, g, b):
    xf = x.astype(jnp.float32)
    mu = jnp.mean(xf, axis=-1, keepdims=True)
    xc = xf - mu
    var = jnp.mean(xc * xc, axis=-1, keepdims=True)
    y = xc * lax.rsqrt(var + EPS) * g.astype(jnp.float32) + b.astype(jnp.float32)
    return y.astype(x.dtype)

def causal_dwconv(x, w):
    k = w.shape[0]
    return lax.conv_general_dilated(
        x, w.astype(x.dtype)[:, None, :],
        window_strides=(1,), padding=[(k - 1, 0)],
        dimension_numbers=("NWC", "WIO", "NWC"),
        feature_group_count=x.shape[-1])

def memory_cross_attention(q, mem_n, w_kv):
    b, s, _ = q.shape
    kv = jnp.einsum("bmd,de->bme", mem_n, w_kv)
    k, v = jnp.split(kv, 2, axis=-1)
    qh = q.reshape(b, s, N_HEADS_X, HEAD_DIM_X)
    kh = k.reshape(b, -1, N_HEADS_X, HEAD_DIM_X)
    vh = v.reshape(b, -1, N_HEADS_X, HEAD_DIM_X)
    scores = jnp.einsum("bshd,bmhd->bhsm", qh, kh).astype(jnp.float32) * (HEAD_DIM_X ** -0.5)
    probs = jax.nn.softmax(scores, axis=-1).astype(q.dtype)
    o = jnp.einsum("bhsm,bmhd->bshd", probs, vh)
    return o.reshape(b, s, W_X)

def setup_inputs(seed: int = 0) -> dict:
    key = jax.random.key(seed)
    ks = jax.random.split(key, 20)
    f32 = jnp.float32
    nrm = lambda k, shape: jax.random.normal(k, shape, f32)
    return {
        "x": nrm(ks[0], (BATCH, SEQ, D_MODEL)),
        "mem": nrm(ks[1], (BATCH, MEM_LEN, D_MODEL)),
        "norm_g": 1.0 + 0.02 * nrm(ks[2], (DEPTH, D_MODEL)),
        "w_in": nrm(ks[3], (DEPTH, D_MODEL, IN_COLS)) * D_MODEL ** -0.5,
        "conv_a_w": nrm(ks[4], (DEPTH, CONV_A, W_A)) * CONV_A ** -0.5,
        "w_out_a": nrm(ks[5], (DEPTH, W_A, D_MODEL)) * W_A ** -0.5,
        "conv_b_w": nrm(ks[6], (DEPTH, CONV_B, W_B)) * CONV_B ** -0.5,
        "conv_b_b": 0.02 * nrm(ks[7], (DEPTH, W_B)),
        "ln_b_g": 1.0 + 0.02 * nrm(ks[8], (DEPTH, W_B)),
        "ln_b_b": 0.02 * nrm(ks[9], (DEPTH, W_B)),
        "w_out_b": nrm(ks[10], (DEPTH, W_B, D_MODEL)) * W_B ** -0.5,
        "mem_norm_g": 1.0 + 0.02 * nrm(ks[11], (DEPTH, D_MODEL)),
        "w_kv": nrm(ks[12], (DEPTH, D_MODEL, 2 * W_X)) * D_MODEL ** -0.5,
        "w_out_x": nrm(ks[13], (DEPTH, W_X, D_MODEL)) * W_X ** -0.5,
        "w_o": nrm(ks[14], (DEPTH, D_MODEL, D_MODEL)) * D_MODEL ** -0.5,
        "final_g": 1.0 + 0.02 * nrm(ks[15], (D_MODEL,)),
    }

def reference(x, mem, norm_g, w_in, conv_a_w, w_out_a, conv_b_w, conv_b_b,
              ln_b_g, ln_b_b, w_out_b, mem_norm_g, w_kv, w_out_x, w_o, final_g):
    h = x
    for l in range(DEPTH):
        u = rmsnorm(h, norm_g[l])
        proj = jnp.einsum("bsd,de->bse", u, w_in[l])
        (b_a, c_a, xin_a, z_a,
         val_b, gate_b, z_b,
         q_x, z_x,
         g_a, g_b, g_x) = jnp.split(proj, SPLIT_POINTS, axis=-1)

        ya = b_a * causal_dwconv(c_a * xin_a, conv_a_w[l])
        ya = jnp.einsum("bsc,cd->bsd", jax.nn.silu(z_a) * ya, w_out_a[l])

        yb = val_b * jax.nn.sigmoid(gate_b)
        yb = causal_dwconv(yb, conv_b_w[l]) + conv_b_b[l].astype(yb.dtype)
        yb = jax.nn.silu(layernorm(yb, ln_b_g[l], ln_b_b[l]))
        yb = jnp.einsum("bsc,cd->bsd", jax.nn.silu(z_b) * yb, w_out_b[l])

        mem_n = rmsnorm(mem, mem_norm_g[l])
        yx = memory_cross_attention(q_x, mem_n, w_kv[l])
        yx = jnp.einsum("bsc,cd->bsd", jax.nn.silu(z_x) * yx, w_out_x[l])

        merged = jax.nn.sigmoid(g_a) * ya + jax.nn.sigmoid(g_b) * yb + jax.nn.sigmoid(g_x) * yx
        h = h + jnp.einsum("bsd,de->bse", merged, w_o[l])
    return rmsnorm(h, final_g)


_drawn_inputs = setup_inputs


def setup_inputs(seed=0):
    import zlib

    import numpy as np

    out = dict(_drawn_inputs(seed))
    spreads = {}
    factors = {'norm_g': 4.085,
     'conv_b_b': 63.696,
     'ln_b_g': 64.0,
     'ln_b_b': 64.0,
     'mem_norm_g': 34.741,
     'final_g': 8.187}
    for name, (base, spread) in spreads.items():
        noise = np.random.default_rng([zlib.crc32(name.encode()), seed]).standard_normal(out[name].shape)
        drawn = base * np.exp(spread * noise) if base else spread * noise
        out[name] = __import__('jax').numpy.asarray(drawn.astype(out[name].dtype))
    for name, factor in factors.items():
        out[name] = (out[name] * factor).astype(out[name].dtype)
    return out
```

```python
import numpy as np

import concourse.bass as bass
from concourse import mybir

P = 128
D = 1024
S = 1024
MEM = 256
KB = D // P
SB = S // P
MB = MEM // P
HALF = 512
HEADS = 4
HEAD_DIM = D // HEADS
TAPS_A = 3
TAPS_B = 31
PAD_A = TAPS_A - 1
PAD_B = TAPS_B - 1
EPS = 1e-6
SCALE = float(HEAD_DIM) ** -0.5

COL_B_A, COL_C_A, COL_X_A, COL_Z_A, COL_VAL_B, COL_GATE_B, COL_Z_B, COL_Q, COL_Z_X, COL_G_A, COL_G_B, COL_G_X = range(12)

Q_B_IN = 0
Q_A_IN = Q_B_IN + KB
Q_A_OUT = Q_A_IN + 2 * KB
Q_B_Z = Q_A_OUT + KB
Q_B_OUT = Q_B_Z + KB // 2
Q_ATT = Q_B_OUT + KB
Q_G_X = Q_ATT + 4 * HEADS
Q_X_OUT = Q_G_X + KB // 2
Q_FINAL = Q_X_OUT + KB // 2

PC_CONV_B = 0
PC_CONV_A = 256
PC_NORM_G = PC_CONV_A + TAPS_A * KB
PC_CONV_BIAS = PC_NORM_G + KB
PC_LN_G = PC_CONV_BIAS + KB
PC_LN_B = PC_LN_G + KB
PC_MEM_G = PC_LN_B + KB
PC_END = PC_MEM_G + KB

MEM_ORDER = list(range(0, KB, 2)) + list(range(1, KB, 2))

F32 = mybir.dt.float32
F32R = mybir.dt.float32r
ACT = mybir.ActivationFunctionType
ALU = mybir.AluOpType
AX = mybir.AxisListType


def build(nc, x, mem, norm_g, w_in, conv_a_w, w_out_a, conv_b_w, conv_b_b, ln_b_g, ln_b_b, w_out_b,
          mem_norm_g, w_kv, w_out_x, w_o, final_g, out):
    from contextlib import ExitStack

    ctx = ExitStack()
    with ctx:
        place = [(nc.sbuf_base + 31) // 32 * 32]

        def sbuf(name, shape, dtype, at=None):
            size = int(np.prod(shape[1:])) * 4
            offset = place[0] if at is None else at
            tensor = nc.alloc_sbuf_tensor_at(name, shape, dtype, offset=offset)
            if at is None:
                place[0] += (size + 31) // 32 * 32
            return tensor

        u_hi = sbuf("u_hi", [P, KB, S], F32R)
        u_lo = sbuf("u_lo", [P, KB, S], F32R)
        y_hi = sbuf("y_hi", [P, KB, S], F32R)
        y_lo = sbuf("y_lo", [P, KB, S], F32R)
        raw = sbuf("raw", [P, 2, S], F32)
        w_hi = sbuf("w_hi", [P, 2, S], F32R)
        w_lo = sbuf("w_lo", [P, 2, S], F32R)
        tile = sbuf("tile", [P, 2, S], F32)
        side = sbuf("side", [P, 2, S + 4], F32)
        shared = place[0]
        glu = sbuf("glu", [P, KB, PAD_B + S], F32)
        mem_hi = sbuf("mem_hi", [P, KB, MEM], F32R, at=shared)
        mem_lo = sbuf("mem_lo", [P, KB, MEM], F32R, at=shared + 8192)
        k_hi = sbuf("k_hi", [P, 2, MEM], F32R, at=shared + 16384)
        k_lo = sbuf("k_lo", [P, 2, MEM], F32R, at=shared + 18432)
        v_hi = sbuf("v_hi", [P, MB, HEAD_DIM], F32R, at=shared + 20480)
        v_lo = sbuf("v_lo", [P, MB, HEAD_DIM], F32R, at=shared + 22528)
        merged = sbuf("merged", [P, KB, S], F32, at=shared)
        ident = sbuf("ident", [P, P], F32)
        ones = sbuf("ones", [P, P], F32)
        param = sbuf("param", [P, PC_END], F32)
        eps = sbuf("eps", [P, 1], F32)
        stat = sbuf("stat", [P, 48], F32)
        sumsq = stat[:, 0:8]
        rootms = stat[:, 8:16]
        rstd = stat[:, 16:24]
        peak = stat[:, 24:32]
        negpeak = stat[:, 32:40]
        rowsum = stat[:, 40:48]
        assert place[0] <= nc.sbuf_usable_end, place[0]

        def half(b):
            return slice(b * HALF, (b + 1) * HALF)

        def psum(name):
            return ctx.enter_context(nc.psum_tensor(name, [P, S], F32))

        pair = [psum("pair0"), psum("pair1")]
        misc = ctx.enter_context(nc.psum_tensor("misc", [P, 4, HALF], F32))
        score = misc[:, :, :].rearrange("p b (s m) -> p (b s) m", m=MEM)
        misc2 = misc[:, :, :].rearrange("p (a b) f -> p a (b f)", a=2)
        prob = side[:, :, 0:S].rearrange("p a (s m) -> p a s m", m=MEM)

        part_a = nc.dram_tensor("part_a", (KB, P, S), F32).ap()
        part_b = nc.dram_tensor("part_b", (KB, P, S), F32).ap()

        def sem(name):
            return ctx.enter_context(nc.semaphore(name))

        def sem2(name):
            return [sem(name + "0"), sem(name + "1")]

        raw_loaded = sem2("raw_loaded")
        hi_done = sem2("hi_done")
        lo_done = sem2("lo_done")
        step_done = sem2("step_done")
        x_loaded = [sem(f"x_loaded{b}") for b in range(SB)]
        param_loaded = sem("param_loaded")
        const_done = sem("const_done")
        fills = sem("fills")
        param_turned = sem("param_turned")
        param_copied = sem("param_copied")
        sq_done = sem("sq_done")
        root_done = sem("root_done")
        rstd_done = sem("rstd_done")
        x_scaled = sem("x_scaled")
        x_turned = sem("x_turned")
        u_hi_done = sem("u_hi_done")
        u_lo_done = sem("u_lo_done")
        gate_b_done = sem("gate_b_done")
        glu_done = sem("glu_done")
        conv_taps = sem("conv_taps")
        ln_sum = sem("ln_sum")
        mean_done = sem("mean_done")
        ln_centered = sem("ln_centered")
        ln_squared = sem("ln_squared")
        ln_sqsum = sem("ln_sqsum")
        var_done = sem("var_done")
        ln_root = sem("ln_root")
        ln_rstd = sem("ln_rstd")
        ln_scaled = sem("ln_scaled")
        z_b_done = sem2("z_b_done")
        ln_swished = sem("ln_swished")
        y_b_product = sem("y_b_product")
        y_b_hi = sem("y_b_hi")
        y_b_lo = sem("y_b_lo")
        c_a_copied = sem("c_a_copied")
        cx_done = sem("cx_done")
        conv_a_done = sem("conv_a_done")
        b_a_done = sem("b_a_done")
        z_a_done = sem("z_a_done")
        y_a_product = sem("y_a_product")
        y_a_hi = sem("y_a_hi")
        y_a_lo = sem("y_a_lo")
        gate_done = {"a": sem("gate_a_done"), "b": sem("gate_b_out_done")}
        gated = {"a": sem("gated_a"), "b": sem("gated_b")}
        stored = {"a": sem2("stored_a"), "b": sem2("stored_b")}
        mem_loaded = sem2("mem_loaded")
        mem_sq = sem("mem_sq")
        mem_root = sem("mem_root")
        mem_rstd = sem("mem_rstd")
        mem_scaled = sem("mem_scaled")
        mem_turned = sem("mem_turned")
        mem_hi_done = sem("mem_hi_done")
        mem_lo_done = sem("mem_lo_done")
        k_hi_done = sem("k_hi_done")
        k_lo_done = sem("k_lo_done")
        q_hi_done = sem("q_hi_done")
        q_lo_done = sem("q_lo_done")
        v_hi_done = sem("v_hi_done")
        v_lo_done = sem("v_lo_done")
        z_x_done = sem("z_x_done")
        scores_done = sem("scores_done")
        peak_done = sem("peak_done")
        negpeak_done = sem("negpeak_done")
        exp_done = sem("exp_done")
        denom_done = sem("denom_done")
        prob_done = sem("prob_done")
        prob_turned = sem("prob_turned")
        pt_hi_done = sem("pt_hi_done")
        pt_lo_done = sem("pt_lo_done")
        pv_done = sem("pv_done")
        y_x_product = sem("y_x_product")
        y_x_hi = sem("y_x_hi")
        y_x_lo = sem("y_x_lo")
        gate_x_done = sem2("gate_x_done")
        parts_loaded = sem2("parts_loaded")
        parts_added = sem("parts_added")
        gated_x = sem2("gated_x")
        merged_done = sem2("merged_done")
        wo_hi_done = sem("wo_hi_done")
        wo_lo_done = sem("wo_lo_done")
        xres_loaded = sem2("xres_loaded")
        fg_loaded = sem("fg_loaded")
        resid_done = sem2("resid_done")
        out_sq = sem("out_sq")
        out_root = sem("out_root")
        out_rstd = sem("out_rstd")
        out_ready = sem2("out_ready")
        out_stored = sem2("out_stored")

        w_in_t = w_in[0].rearrange("(k p) (g e) -> p k g e", p=P, e=P)
        w_kv_t = w_kv[0].rearrange("(k p) (g e) -> p k g e", p=P, e=P)
        w_out_t = {n: w[0].rearrange("(k p) (g e) -> p k g e", p=P, e=P)
                   for n, w in (("a", w_out_a), ("b", w_out_b), ("x", w_out_x))}
        w_o_rows = w_o[0].rearrange("(k p) e -> k p e", p=P)
        x_blocks = x[0].rearrange("(b p) d -> b p d", p=P)
        mem_blocks = mem[0].rearrange("(b p) d -> b p d", p=P)
        out_blocks = out[0].rearrange("(b p) d -> b p d", p=P)

        block = ctx.enter_context(nc.Block())

        @block.sync
        def _(sp):
            rows = raw
            conv_b_rows = conv_b_w[0].rearrange("j (k c) -> (j k) c", c=P)
            sp.dma_start(rows[:, 0, 0:P], conv_b_rows[0:P]).then_inc(param_loaded, 16)
            sp.dma_start(rows[0:TAPS_B * KB - P, 0, P:2 * P], conv_b_rows[P:TAPS_B * KB]).then_inc(param_loaded, 16)
            at = 0
            for source, n in ((conv_a_w[0].rearrange("j (k c) -> (j k) c", c=P), TAPS_A * KB),
                              (norm_g.rearrange("l (k c) -> (l k) c", c=P), KB),
                              (conv_b_b.rearrange("l (k c) -> (l k) c", c=P), KB),
                              (ln_b_g.rearrange("l (k c) -> (l k) c", c=P), KB),
                              (ln_b_b.rearrange("l (k c) -> (l k) c", c=P), KB),
                              (mem_norm_g.rearrange("l (k c) -> (l k) c", c=P), KB)):
                sp.dma_start(rows[at:at + n, 0, 2 * P:3 * P], source).then_inc(param_loaded, 16)
                at += n
            for b in range(SB):
                sp.dma_start(glu[:, b, PAD_B:], x_blocks[b]).then_inc(x_loaded[b], 16)

            def load(slot, count, source):
                sp.wait_ge(lo_done[slot], count)
                sp.dma_start(raw[:, slot, :].rearrange("p (k e) -> p k e", e=P), source).then_inc(raw_loaded[slot], 16)

            sp.wait_ge(param_turned, 3)
            with sp.Fori(0, KB) as c:
                load(0, Q_B_IN + c, w_in_t[:, :, COL_VAL_B * KB + c, :])
                load(1, Q_B_IN + c, w_in_t[:, :, COL_GATE_B * KB + c, :])
            with sp.Fori(0, KB) as c:
                load(0, Q_A_IN + c * 2, w_in_t[:, :, COL_C_A * KB + c, :])
                load(1, Q_A_IN + c * 2, w_in_t[:, :, COL_X_A * KB + c, :])
                load(0, Q_A_IN + c * 2 + 1, w_in_t[:, :, COL_B_A * KB + c, :])
                load(1, Q_A_IN + c * 2 + 1, w_in_t[:, :, COL_Z_A * KB + c, :])
            with sp.Fori(0, KB) as d:
                load(0, Q_A_OUT + d, w_in_t[:, :, COL_G_A * KB + d, :])
                load(1, Q_A_OUT + d, w_out_t["a"][:, :, d, :])
            with sp.Fori(0, KB // 2) as i:
                load(0, Q_B_Z + i, w_in_t[:, :, COL_Z_B * KB + i * 2, :])
                load(1, Q_B_Z + i, w_in_t[:, :, COL_Z_B * KB + i * 2 + 1, :])
            load(0, Q_B_OUT, w_in_t[:, :, COL_G_B * KB, :])
            load(1, Q_B_OUT, w_out_t["b"][:, :, 0, :])
            for b in range(MB):
                sp.wait_ge(ln_scaled, KB)
                sp.dma_start(side[:, b, 0:D], mem_blocks[b]).then_inc(mem_loaded[b], 16)
            with sp.Fori(1, KB) as d:
                load(0, Q_B_OUT + d, w_in_t[:, :, COL_G_B * KB + d, :])
                load(1, Q_B_OUT + d, w_out_t["b"][:, :, d, :])
            with sp.Fori(0, HEADS) as h:
                q = Q_ATT + h * 4
                load(0, q, w_kv_t[:, :, h * 2, :])
                load(1, q, w_in_t[:, :, COL_Q * KB + h * 2, :])
                load(0, q + 1, w_kv_t[:, :, h * 2 + 1, :])
                load(1, q + 1, w_in_t[:, :, COL_Q * KB + h * 2 + 1, :])
                load(0, q + 2, w_kv_t[:, :, KB + h * 2, :])
                load(1, q + 2, w_in_t[:, :, COL_Z_X * KB + h * 2, :])
                load(0, q + 3, w_kv_t[:, :, KB + h * 2 + 1, :])
                load(1, q + 3, w_in_t[:, :, COL_Z_X * KB + h * 2 + 1, :])
            with sp.Fori(0, KB // 2) as i:
                load(0, Q_G_X + i, w_in_t[:, :, COL_G_X * KB + i * 2, :])
                load(1, Q_G_X + i, w_in_t[:, :, COL_G_X * KB + i * 2 + 1, :])
            sp.wait_ge(y_x_lo, 2 * HEADS)
            sp.wait_ge(prob_turned, HEADS)
            with sp.Fori(0, KB // 2) as i:
                for s in range(2):
                    d = i * 2 + s
                    sp.wait_ge(lo_done[1 - s], Q_X_OUT + i + s)
                    if s == 0:
                        sp.wait_ge(lo_done[0], Q_X_OUT + i)
                    sp.dma_start(raw[:, 0, :].rearrange("p (k e) -> p k e", e=P), w_out_t["x"][:, :, d, :]).then_inc(raw_loaded[0], 16)
                    sp.wait_ge(wo_lo_done, d)
                    sp.dma_start(raw[:, 1, :], w_o_rows[d]).then_inc(raw_loaded[1], 16)
                    sp.wait_ge(merged_done[s], i)
                    sp.dma_start(tile[:, s, :], part_a[d]).then_inc(parts_loaded[s], 16)
                    sp.dma_start(side[:, s, 0:S], part_b[d]).then_inc(parts_loaded[s], 16)
            sp.wait_ge(lo_done[1], Q_FINAL)
            sp.wait_ge(wo_lo_done, KB)
            sp.wait_ge(merged_done[1], KB // 2)
            sp.dma_start(side[:, 0, 0:D], final_g.rearrange("(a d) -> a d", a=1).to_broadcast([P, D])).then_inc(fg_loaded, 16)
            with sp.Fori(0, SB // 2) as i:
                for s in range(2):
                    sp.wait_ge(out_ready[s], i)
                    sp.dma_start(raw[:, s, :], x_blocks[i * 2 + s]).then_inc(xres_loaded[s], 16)
            for s in range(2):
                sp.wait_ge(out_stored[s], 16 * (SB // 2))

        @block.gpsimd
        def _(pool):
            nc.gpsimd.memset(ident[:], 0.0).then_inc(const_done, 1)
            pool.wait_ge(const_done, 1)
            nc.gpsimd.affine_select(out=ident[:], in_=ident[:], compare_op=ALU.not_equal, fill=1.0, base=0,
                                    pattern=[[-1, P]], channel_multiplier=1).then_inc(const_done, 1)

        @block.scalar
        def _(act):
            def w_round(slot, count):
                act.wait_ge(raw_loaded[slot], count * 16 + 16)
                act.wait_ge(step_done[slot], count)
                act.activation(w_hi[:, slot, :], raw[:, slot, :], ACT.Copy).then_inc(hi_done[slot], 1)

            for g in range(2):
                for b in range(4 * g, 4 * g + 4):
                    act.wait_ge(x_loaded[b], 16)
                    act.wait_ge(sq_done, b)
                    act.activation(tile[:, 0, :], glu[:, b, PAD_B:], ACT.Square,
                                   accum_out=sumsq[:, b:b + 1]).then_inc(sq_done, 1)
                act.wait_ge(sq_done, 4 * g + 4)
                act.wait_ge(fills, 2)
                act.activation(rootms[:, 4 * g:4 * g + 4], sumsq[:, 4 * g:4 * g + 4], ACT.Sqrt,
                               scale=1.0 / D, bias=eps[:, 0:1]).then_inc(root_done, 1)
            act.wait_ge(param_copied, 2)
            for g in range(2):
                for k in range(KB):
                    n = g * KB + k
                    act.wait_ge(x_turned, n + 1)
                    act.activation(u_hi[:, k, half(g)], misc[:, n % 4, :], ACT.Copy,
                                   scale=param[:, PC_NORM_G + k:PC_NORM_G + k + 1]).then_inc(u_hi_done, 1)
                if g == 0:
                    w_round(0, 0)
                    w_round(1, 0)

            with act.Fori(0, KB) as c:
                w_round(0, Q_B_IN + c + 1)
                w_round(1, Q_B_IN + c + 1)
                act.wait_ge(step_done[1], Q_B_IN + c + 1)
                act.wait_ge(glu_done, c)
                act.activation(tile[:, 0, :], pair[1][:], ACT.Sigmoid).then_inc(gate_b_done, 1)

            act.wait_ge(conv_taps, 2 * TAPS_B)
            with act.Fori(0, KB) as c:
                q = Q_A_IN + c * 2
                w_round(0, q + 1)
                act.wait_ge(y_a_product, c)
                act.activation(tile[:, 0, :], pair[0][:], ACT.Copy).then_inc(c_a_copied, 1)
                w_round(1, q + 1)
                w_round(0, q + 2)
                w_round(1, q + 2)
                act.wait_ge(y_a_lo, c)
                act.activation(tile[:, 1, :], pair[1][:], ACT.Silu).then_inc(z_a_done, 1)
                act.wait_ge(y_a_product, c + 1)
                act.activation(y_hi[:, c, :], tile[:, 1, :], ACT.Copy).then_inc(y_a_hi, 1)

            def gate_out(branch, q, i, s):
                d = i * 2 + s
                part = part_a if branch == "a" else part_b
                w_round(0, q + d + 1)
                act.wait_ge(stored[branch][s], i * 16)
                act.activation(tile[:, s, :], pair[0][:], ACT.Sigmoid).then_inc(gate_done[branch], 1)
                w_round(1, q + d + 1)
                act.wait_ge(gated[branch], d + 1)
                act.dma_start(part[d], tile[:, s, :]).then_inc(stored[branch][s], 16)

            act.wait_ge(y_a_lo, KB)
            with act.Fori(0, 3) as i:
                for s in range(2):
                    gate_out("a", Q_A_OUT, i, s)
            for s in range(2):
                gate_out("a", Q_A_OUT, 3, s)
                for c in range(4 * s, 4 * s + 4):
                    act.wait_ge(ln_centered, c + 1)
                    act.wait_ge(ln_sqsum, c)
                    act.activation(misc2[:, 1, :], glu[:, c, PAD_B:], ACT.Square).then_inc(ln_squared, 1)

            w_round(0, Q_B_Z + 1)
            act.wait_ge(var_done, 1)
            act.activation(side[:, 0, 0:S], misc2[:, 0, :], ACT.Sqrt, bias=eps[:, 0:1]).then_inc(ln_root, 1)
            act.wait_ge(stored["a"][0], 64)
            act.wait_ge(stored["a"][1], 64)

            def z_b(i, s):
                c = i * 2 + s
                act.wait_ge(step_done[s], Q_B_Z + i + 1)
                if s == 0:
                    act.wait_ge(y_b_lo, i * 2)
                act.activation(tile[:, s, :], pair[s][:], ACT.Silu).then_inc(z_b_done[s], 1)
                act.wait_ge(ln_scaled, c + 1)
                act.activation(glu[:, c, PAD_B:], glu[:, c, PAD_B:], ACT.Silu,
                               scale=param[:, bass.ds(c + PC_LN_G, 1)],
                               bias=param[:, bass.ds(c + PC_LN_B, 1)]).then_inc(ln_swished, 1)
                act.wait_ge(y_b_product, c + 1)
                act.activation(y_hi[:, c, :], tile[:, s, :], ACT.Copy).then_inc(y_b_hi, 1)

            z_b(0, 0)
            w_round(1, Q_B_Z + 1)
            z_b(0, 1)
            with act.Fori(1, KB // 2) as i:
                w_round(0, Q_B_Z + i + 1)
                z_b(i, 0)
                w_round(1, Q_B_Z + i + 1)
                z_b(i, 1)

            for b in range(MB):
                act.wait_ge(mem_loaded[b], 16)
                act.wait_ge(y_b_lo, KB)
                act.activation(misc2[:, b, :], side[:, b, 0:D], ACT.Square,
                               accum_out=sumsq[:, b:b + 1]).then_inc(mem_sq, 1)
            act.wait_ge(mem_sq, MB)
            act.activation(rootms[:, 0:MB], sumsq[:, 0:MB], ACT.Sqrt, scale=1.0 / D,
                           bias=eps[:, 0:1]).then_inc(mem_root, 1)
            with act.Fori(0, 2) as i:
                for s in range(2):
                    gate_out("b", Q_B_OUT, i, s)
            act.wait_ge(mem_turned, 1)
            for n, k in enumerate(MEM_ORDER):
                if n >= 4:
                    act.wait_ge(mem_lo_done, n - 3)
                act.activation(mem_hi[:, k, :], score[:, k, :], ACT.Copy,
                               scale=param[:, PC_MEM_G + k:PC_MEM_G + k + 1]).then_inc(mem_hi_done, 1)
            with act.Fori(2, 4) as i:
                for s in range(2):
                    gate_out("b", Q_B_OUT, i, s)

            act.wait_ge(stored["b"][0], 64)
            act.wait_ge(stored["b"][1], 64)
            with act.Fori(0, HEADS) as h:
                q = Q_ATT + h * 4

                def k_round(j):
                    w_round(0, q + j + 1)
                    act.activation(k_hi[:, j, :], pair[0][:, 0:MEM], ACT.Copy).then_inc(k_hi_done, 1)

                def q_round(j):
                    w_round(1, q + j + 1)
                    act.activation(y_hi[:, KB - 2 + j, :], pair[1][:], ACT.Copy).then_inc(q_hi_done, 1)

                def v_round(j):
                    w_round(0, q + j + 3)
                    act.activation(v_hi[:, :, j * P:(j + 1) * P],
                                   pair[0][:].rearrange("p (b f) -> p b f", b=2)[:, :, 0:P],
                                   ACT.Copy).then_inc(v_hi_done, 1)

                def z_x(j):
                    w_round(1, q + j + 3)
                    act.wait_ge(y_x_lo, h * 2)
                    act.activation(tile[:, j, :], pair[1][:], ACT.Silu).then_inc(z_x_done, 1)

                k_round(0)
                q_round(0)
                k_round(1)
                q_round(1)
                v_round(0)
                act.wait_ge(negpeak_done, h + 1)
                for b in range(SB):
                    act.activation(prob[:, b // 4, b % 4, :], score[:, b, :], ACT.Exp, scale=SCALE,
                                   bias=negpeak[:, b:b + 1], accum_out=rowsum[:, b:b + 1]).then_inc(exp_done, 1)
                z_x(0)
                v_round(1)
                for b in range(MB):
                    act.wait_ge(prob_turned, h + 1)
                    act.activation(y_hi[:, KB - 2 + b, :], misc2[:, b, :], ACT.Copy).then_inc(pt_hi_done, 1)
                z_x(1)
                act.wait_ge(y_x_product, h * 2 + 2)
                for j in range(2):
                    act.activation(y_hi[:, h * 2 + j, :], tile[:, j, :], ACT.Copy).then_inc(y_x_hi, 1)

            def tile_round(slot, count, d):
                act.wait_ge(raw_loaded[0], (d + (Q_X_OUT + 1)) * 16)
                act.wait_ge(step_done[slot], count)
                act.activation(w_hi[:, slot, :], raw[:, 0, :], ACT.Copy).then_inc(hi_done[slot], 1)

            def gate_x(i, s):
                act.wait_ge(step_done[s], i + (Q_G_X + 1))
                act.activation(merged[:, i * 2 + s, :], pair[s][:], ACT.Sigmoid).then_inc(gate_x_done[s], 1)

            with act.Fori(0, KB // 2 - 1) as i:
                for s in range(2):
                    w_round(s, i + (Q_G_X + 1))
                    gate_x(i, s)
            for s in range(2):
                tile_round(s, Q_X_OUT, s)
                gate_x(KB // 2 - 1, s)

            def wo_round(d):
                act.wait_ge(raw_loaded[1], (d + (Q_X_OUT + 1)) * 16)
                act.wait_ge(step_done[1], Q_X_OUT)
                act.activation(u_hi[:, d, :], raw[:, 1, :], ACT.Copy).then_inc(wo_hi_done, 1)

            with act.Fori(0, KB // 2 - 1) as i:
                for s in range(2):
                    wo_round(i * 2 + s)
                    tile_round(s, i + (Q_X_OUT + 1), i * 2 + s + 2)
            for s in range(2):
                wo_round(KB - 2 + s)

            def merged_round(i, s):
                act.wait_ge(step_done[s], i + Q_FINAL)
                act.activation(w_hi[:, s, :].rearrange("p (k e) -> p k e", e=P),
                               merged[:, :, bass.ds((i * 2 + s) * P, P)], ACT.Copy).then_inc(hi_done[s], 1)

            for s in range(2):
                act.wait_ge(merged_done[s], KB // 2)
            for s in range(2):
                merged_round(0, s)

            def finish(i, s):
                b = i * 2 + s
                act.wait_ge(resid_done[s], i + 1)
                act.activation(misc2[:, s, :], raw[:, s, :], ACT.Square,
                               accum_out=sumsq[:, bass.ds(b, 1)]).then_inc(out_sq, 1)
                act.wait_ge(out_sq, b + 1)
                act.activation(rootms[:, bass.ds(b, 1)], sumsq[:, bass.ds(b, 1)], ACT.Sqrt, scale=1.0 / D,
                               bias=eps[:, 0:1]).then_inc(out_root, 1)
                act.wait_ge(out_ready[s], i + 1)
                act.dma_start(out_blocks[b], tile[:, s, :]).then_inc(out_stored[s], 16)

            with act.Fori(0, SB // 2 - 1) as i:
                for s in range(2):
                    merged_round(i + 1, s)
                    finish(i, s)
            for s in range(2):
                finish(SB // 2 - 1, s)

        @block.vector
        def _(dve):
            def w_rest(slot, count):
                dve.wait_ge(hi_done[slot], count + 1)
                dve.tensor_tensor(w_lo[:, slot, :], raw[:, slot, :], w_hi[:, slot, :].bitcast(F32),
                                  ALU.subtract).then_inc(lo_done[slot], 1)

            dve.memset(eps[:], EPS).then_inc(fills, 1)
            dve.memset(ones[:], 1.0 / D).then_inc(fills, 1)
            dve.memset(glu[:, :, 0:PAD_B], 0.0).then_inc(fills, 1)
            dve.memset(side[:, 1, 0:PAD_A], 0.0).then_inc(fills, 1)
            dve.wait_ge(param_turned, 3)
            dve.tensor_copy(param[:, 0:TAPS_B * KB], pair[0][:, 0:TAPS_B * KB]).then_inc(param_copied, 1)
            dve.tensor_copy(param[:, PC_CONV_A:PC_END], pair[0][:, PC_CONV_A:PC_END]).then_inc(param_copied, 1)
            dve.wait_ge(param_copied, 2)
            dve.wait_ge(fills, 4)
            for g in range(2):
                dve.wait_ge(root_done, g + 1)
                dve.reciprocal(rstd[:, 4 * g:4 * g + 4], rootms[:, 4 * g:4 * g + 4]).then_inc(rstd_done, 1)
                dve.wait_ge(rstd_done, g + 1)
                for b in range(4 * g, 4 * g + 4):
                    dve.tensor_scalar(glu[:, b, PAD_B:], glu[:, b, PAD_B:], rstd[:, b:b + 1], None,
                                      ALU.mult).then_inc(x_scaled, 1)
            for g in range(2):
                for k in range(KB):
                    n = g * KB + k
                    dve.wait_ge(u_hi_done, n + 1)
                    dve.scalar_tensor_tensor(out=u_lo[:, k, half(g)], in0=misc[:, n % 4, :],
                                             scalar=param[:, PC_NORM_G + k:PC_NORM_G + k + 1],
                                             in1=u_hi[:, k, half(g)].bitcast(F32), op0=ALU.mult,
                                             op1=ALU.subtract).then_inc(u_lo_done, 1)
                if g == 0:
                    w_rest(0, 0)
                    w_rest(1, 0)

            def conv_tap(c, tap, sums, done, source=None):
                dve.wait_ge(conv_taps, done)
                weight = param[:, bass.ds(tap * KB + c + PC_CONV_B, 1)]
                if source is not None:
                    dve.scalar_tensor_tensor(out=sums, in0=source, scalar=weight, in1=sums, op0=ALU.mult,
                                             op1=ALU.add).then_inc(conv_taps, 1)
                elif tap == 0:
                    dve.tensor_scalar(sums, glu[:, c, 0:S], weight, param[:, bass.ds(c + PC_CONV_BIAS, 1)],
                                      ALU.mult, ALU.add).then_inc(conv_taps, 1)
                elif tap < TAPS_B - 1:
                    dve.scalar_tensor_tensor(out=sums, in0=glu[:, c, tap:tap + S], scalar=weight, in1=sums,
                                             op0=ALU.mult, op1=ALU.add).then_inc(conv_taps, 1)
                else:
                    dve.scalar_tensor_tensor(out=glu[:, c, PAD_B:], in0=glu[:, c, PAD_B:], scalar=weight,
                                             in1=sums, op0=ALU.mult, op1=ALU.add).then_inc(conv_taps, 1)

            def two_convs(c, taps, sums, base):
                for tap in taps:
                    for s in range(2):
                        conv_tap(c + s, tap, sums[s], base + max(2 * tap + s - 1, 0))

            def two_convs_at(c, first, n, sums, done):
                for t in range(n):
                    for s in range(2):
                        conv_tap(c + s, first + t, sums[s], done + (2 * t + s),
                                 source=glu[:, c + s, bass.ds(first + t, S)])

            def b_in(c, taps=lambda part: None):
                w_rest(0, c + (Q_B_IN + 1))
                taps(0)
                w_rest(1, c + (Q_B_IN + 1))
                dve.wait_ge(gate_b_done, c + 1)
                dve.tensor_tensor(glu[:, c, PAD_B:], pair[0][:], tile[:, 0, :], ALU.mult).then_inc(glu_done, 1)
                taps(1)

            sums_b_in = [side[:, 0, 0:S], tile[:, 1, :]]
            with dve.Fori(0, 2) as c:
                b_in(c)
            dve.wait_ge(glu_done, 2)
            two_convs(0, [0], sums_b_in, 0)
            with dve.Fori(0, 4) as i:
                b_in(i + 2, lambda part: two_convs_at(0, i * 7 + (4 * part + 1), 4 - part, sums_b_in,
                                                      i * 14 + (8 * part + 1)))
            b_in(6, lambda part: two_convs(0, [29 + part], sums_b_in, 0))
            b_in(7)

            taps_before = 2 * TAPS_B
            dve.wait_ge(glu_done, KB)
            with dve.Fori(0, KB // 2) as i:
                for s in range(2):
                    c = i * 2 + s
                    q = c * 2 + Q_A_IN

                    def taps(part):
                        each = 4
                        for tap in range(16 * s + each * part, min(16 * s + each * part + each, TAPS_B)):
                            conv_tap(i + 2, tap, side[:, 0, 0:S], i * TAPS_B + (taps_before + tap))

                    w_rest(0, q + 1)
                    taps(0)
                    w_rest(1, q + 1)
                    dve.wait_ge(step_done[1], q + 1)
                    dve.wait_ge(c_a_copied, c + 1)
                    dve.wait_ge(conv_a_done, c * TAPS_A)
                    dve.tensor_tensor(side[:, 1, PAD_A:PAD_A + S], pair[1][:], tile[:, 0, :],
                                      ALU.mult).then_inc(cx_done, 1)
                    dve.wait_ge(cx_done, c + 1)
                    for tap in range(TAPS_A):
                        weight = param[:, bass.ds(c + (PC_CONV_A + tap * KB), 1)]
                        dve.wait_ge(conv_a_done, c * TAPS_A + tap)
                        if tap == 0:
                            dve.tensor_scalar(tile[:, 0, :], side[:, 1, 0:S], weight, None,
                                              ALU.mult).then_inc(conv_a_done, 1)
                        else:
                            dve.scalar_tensor_tensor(out=tile[:, 0, :], in0=side[:, 1, tap:tap + S],
                                                     scalar=weight, in1=tile[:, 0, :], op0=ALU.mult,
                                                     op1=ALU.add).then_inc(conv_a_done, 1)
                    taps(1)
                    w_rest(0, q + 2)
                    dve.wait_ge(step_done[0], q + 2)
                    dve.wait_ge(conv_a_done, c * TAPS_A + TAPS_A)
                    dve.tensor_tensor(tile[:, 0, :], pair[0][:], tile[:, 0, :], ALU.mult).then_inc(b_a_done, 1)
                    taps(2)
                    w_rest(1, q + 2)
                    dve.wait_ge(z_a_done, c + 1)
                    dve.wait_ge(b_a_done, c + 1)
                    dve.tensor_tensor(tile[:, 1, :], tile[:, 1, :], tile[:, 0, :], ALU.mult).then_inc(y_a_product, 1)
                    taps(3)
                    dve.wait_ge(y_a_hi, c + 1)
                    dve.tensor_tensor(y_lo[:, c, :], tile[:, 1, :], y_hi[:, c, :].bitcast(F32),
                                      ALU.subtract).then_inc(y_a_lo, 1)

            def gate_out(branch, q, d, s, taps=lambda part: None):
                w_rest(0, d + (q + 1))
                taps(0)
                w_rest(1, d + (q + 1))
                dve.wait_ge(step_done[1], d + (q + 1))
                dve.wait_ge(gate_done[branch], d + 1)
                dve.tensor_tensor(tile[:, s, :], pair[1][:], tile[:, s, :], ALU.mult).then_inc(gated[branch], 1)
                taps(1)

            taps_before = 6 * TAPS_B
            sums_a_out = [side[:, 0, 0:S], side[:, 1, 0:S]]
            dve.wait_ge(conv_a_done, TAPS_A * KB)
            two_convs(6, [0], sums_a_out, taps_before)
            with dve.Fori(0, 2) as i:
                for s in range(2):
                    gate_out("a", Q_A_OUT, i * 2 + s, s,
                             lambda part: two_convs_at(6, i * 14 + (7 * s + 4 * part + 1), 4 - part, sums_a_out,
                                                       i * 28 + (taps_before + 14 * s + 8 * part + 1)))
            gate_out("a", Q_A_OUT, 4, 0, lambda part: two_convs(6, [29 + part], sums_a_out, taps_before))
            gate_out("a", Q_A_OUT, 5, 1)
            dve.wait_ge(conv_taps, KB * TAPS_B)
            dve.tensor_tensor(side[:, 0, 0:S], glu[:, 0, PAD_B:], glu[:, 1, PAD_B:], ALU.add).then_inc(ln_sum, 1)
            for c in range(2, KB):
                dve.wait_ge(ln_sum, c - 1)
                dve.tensor_tensor(side[:, 0, 0:S], side[:, 0, 0:S], glu[:, c, PAD_B:], ALU.add).then_inc(ln_sum, 1)

            def add_square(c):
                dve.wait_ge(ln_squared, c + 1)
                if c == 0:
                    dve.tensor_copy(side[:, 1, 0:S], misc2[:, 1, :]).then_inc(ln_sqsum, 1)
                else:
                    dve.wait_ge(ln_sqsum, c)
                    dve.tensor_tensor(side[:, 1, 0:S], misc2[:, 1, :], side[:, 1, 0:S], ALU.add).then_inc(ln_sqsum, 1)

            for s in range(2):
                gate_out("a", Q_A_OUT, 6 + s, s)
                dve.wait_ge(mean_done, 1)
                for c in range(4 * s, 4 * s + 4):
                    dve.tensor_tensor(glu[:, c, PAD_B:], misc2[:, 0, :], glu[:, c, PAD_B:],
                                      ALU.subtract).then_inc(ln_centered, 1)
                    if c:
                        add_square(c - 1)
            add_square(KB - 1)

            w_rest(0, Q_B_Z + 1)
            dve.wait_ge(ln_root, 1)
            dve.reciprocal(side[:, 1, 0:S], side[:, 0, 0:S]).then_inc(ln_rstd, 1)
            dve.wait_ge(ln_rstd, 1)

            def ln_scale(c):
                dve.scalar_tensor_tensor(out=glu[:, c, PAD_B:], in0=glu[:, c, PAD_B:], scalar=-1.0,
                                         in1=side[:, 1, 0:S], op0=ALU.mult, op1=ALU.mult).then_inc(ln_scaled, 1)

            def z_b(c, i, s, last=False):
                dve.wait_ge(z_b_done[s], i + 1)
                dve.wait_ge(ln_swished, c + 1)
                dve.tensor_tensor(tile[:, s, :], tile[:, s, :], glu[:, c, PAD_B:], ALU.mult).then_inc(y_b_product, 1)
                if not last:
                    ln_scale(c + 1)
                dve.wait_ge(y_b_hi, c + 1)
                dve.tensor_tensor(y_lo[:, c, :], tile[:, s, :], y_hi[:, c, :].bitcast(F32),
                                  ALU.subtract).then_inc(y_b_lo, 1)

            ln_scale(0)
            z_b(0, 0, 0)
            w_rest(1, Q_B_Z + 1)
            z_b(1, 0, 1)
            with dve.Fori(1, KB // 2 - 1) as i:
                for s in range(2):
                    w_rest(s, i + (Q_B_Z + 1))
                    z_b(i * 2 + s, i, s)
            for s in range(2):
                w_rest(s, Q_B_Z + KB // 2)
                z_b(KB - 2 + s, KB // 2 - 1, s, last=(s == 1))

            dve.wait_ge(mem_root, 1)
            dve.reciprocal(rstd[:, 0:MB], rootms[:, 0:MB]).then_inc(mem_rstd, 1)
            dve.wait_ge(mem_rstd, 1)
            for b in range(MB):
                dve.tensor_scalar(side[:, b, 0:D], side[:, b, 0:D], rstd[:, b:b + 1], None,
                                  ALU.mult).then_inc(mem_scaled, 1)
            with dve.Fori(0, 2) as i:
                for s in range(2):
                    gate_out("b", Q_B_OUT, i * 2 + s, s)
            for n, k in enumerate(MEM_ORDER):
                dve.wait_ge(mem_hi_done, n + 1)
                dve.scalar_tensor_tensor(out=mem_lo[:, k, :], in0=score[:, k, :],
                                         scalar=param[:, PC_MEM_G + k:PC_MEM_G + k + 1],
                                         in1=mem_hi[:, k, :].bitcast(F32), op0=ALU.mult,
                                         op1=ALU.subtract).then_inc(mem_lo_done, 1)
            with dve.Fori(2, 4) as i:
                for s in range(2):
                    gate_out("b", Q_B_OUT, i * 2 + s, s)

            with dve.Fori(0, HEADS) as h:
                q = h * 4 + Q_ATT

                def k_rest(j):
                    w_rest(0, q + j + 1)
                    dve.wait_ge(k_hi_done, h * 2 + j + 1)
                    dve.tensor_tensor(k_lo[:, j, :], pair[0][:, 0:MEM], k_hi[:, j, :].bitcast(F32),
                                      ALU.subtract).then_inc(k_lo_done, 1)

                def q_rest(j):
                    w_rest(1, q + j + 1)
                    dve.wait_ge(q_hi_done, h * 2 + j + 1)
                    dve.tensor_tensor(y_lo[:, KB - 2 + j, :], pair[1][:], y_hi[:, KB - 2 + j, :].bitcast(F32),
                                      ALU.subtract).then_inc(q_lo_done, 1)

                def v_rest(j):
                    w_rest(0, q + j + 3)
                    dve.wait_ge(v_hi_done, h * 2 + j + 1)
                    dve.tensor_tensor(v_lo[:, :, j * P:(j + 1) * P],
                                      pair[0][:].rearrange("p (b f) -> p b f", b=2)[:, :, 0:P],
                                      v_hi[:, :, j * P:(j + 1) * P].bitcast(F32),
                                      ALU.subtract).then_inc(v_lo_done, 1)

                k_rest(0)
                q_rest(0)
                k_rest(1)
                q_rest(1)
                v_rest(0)
                dve.wait_ge(scores_done, h + 1)
                dve.tensor_reduce(peak, score[:, :, :], AX.X, ALU.max).then_inc(peak_done, 1)
                dve.wait_ge(peak_done, h + 1)
                dve.tensor_scalar(negpeak, peak, -SCALE, None, ALU.mult).then_inc(negpeak_done, 1)
                dve.wait_ge(exp_done, h * SB + SB)
                dve.reciprocal(rstd[:, 0:SB], rowsum).then_inc(denom_done, 1)
                dve.wait_ge(denom_done, h + 1)
                for b in range(SB):
                    dve.tensor_scalar(prob[:, b // 4, b % 4, :], prob[:, b // 4, b % 4, :], rstd[:, b:b + 1],
                                      None, ALU.mult).then_inc(prob_done, 1)
                w_rest(1, q + 3)
                v_rest(1)
                for b in range(MB):
                    dve.wait_ge(pt_hi_done, h * MB + b + 1)
                    dve.tensor_tensor(y_lo[:, KB - 2 + b, :], misc2[:, b, :], y_hi[:, KB - 2 + b, :].bitcast(F32),
                                      ALU.subtract).then_inc(pt_lo_done, 1)
                w_rest(1, q + 4)
                for j in range(2):
                    dve.wait_ge(pv_done, h * 2 + j + 1)
                    dve.wait_ge(z_x_done, h * 2 + j + 1)
                    dve.tensor_tensor(tile[:, j, :], pair[j][:], tile[:, j, :], ALU.mult).then_inc(y_x_product, 1)
                for j in range(2):
                    dve.wait_ge(y_x_hi, h * 2 + j + 1)
                    dve.tensor_tensor(y_lo[:, h * 2 + j, :], tile[:, j, :], y_hi[:, h * 2 + j, :].bitcast(F32),
                                      ALU.subtract).then_inc(y_x_lo, 1)

            def tile_rest(slot, count):
                dve.wait_ge(hi_done[slot], count + 1)
                dve.tensor_tensor(w_lo[:, slot, :], raw[:, 0, :], w_hi[:, slot, :].bitcast(F32),
                                  ALU.subtract).then_inc(lo_done[slot], 1)

            with dve.Fori(0, KB // 2 - 1) as i:
                for s in range(2):
                    w_rest(s, i + (Q_G_X + 1))
            for s in range(2):
                tile_rest(s, Q_X_OUT)

            def wo_rest(d):
                dve.wait_ge(wo_hi_done, d + 1)
                dve.tensor_tensor(u_lo[:, d, :], raw[:, 1, :], u_hi[:, d, :].bitcast(F32),
                                  ALU.subtract).then_inc(wo_lo_done, 1)

            def merge(i, s):
                d = i * 2 + s
                dve.wait_ge(gate_x_done[s], KB // 2)
                dve.wait_ge(step_done[s], i + (Q_X_OUT + 1))
                dve.tensor_tensor(merged[:, d, :], pair[s][:], merged[:, d, :], ALU.mult).then_inc(gated_x[s], 1)
                dve.wait_ge(parts_added, d + 1)
                dve.wait_ge(gated_x[s], i + 1)
                dve.tensor_tensor(merged[:, d, :], merged[:, d, :], tile[:, s, :], ALU.add).then_inc(merged_done[s], 1)

            def add_parts(i, s):
                dve.wait_ge(parts_loaded[s], i * 32 + 32)
                dve.tensor_tensor(tile[:, s, :], tile[:, s, :], side[:, s, 0:S], ALU.add).then_inc(parts_added, 1)

            with dve.Fori(0, KB // 2 - 1) as i:
                for s in range(2):
                    wo_rest(i * 2 + s)
                    add_parts(i, s)
                    tile_rest(s, i + (Q_X_OUT + 1))
                    merge(i, s)
            for s in range(2):
                wo_rest(KB - 2 + s)
                add_parts(KB // 2 - 1, s)
                merge(KB // 2 - 1, s)

            def merged_rest(i, s):
                dve.wait_ge(hi_done[s], i + (Q_FINAL + 1))
                dve.tensor_tensor(w_lo[:, s, :].rearrange("p (k e) -> p k e", e=P),
                                  merged[:, :, bass.ds((i * 2 + s) * P, P)],
                                  w_hi[:, s, :].rearrange("p (k e) -> p k e", e=P).bitcast(F32),
                                  ALU.subtract).then_inc(lo_done[s], 1)

            for s in range(2):
                merged_rest(0, s)

            def finish(i, s):
                b = i * 2 + s
                dve.wait_ge(xres_loaded[s], i * 16 + 16)
                dve.wait_ge(step_done[s], i + (Q_FINAL + 1))
                dve.tensor_tensor(raw[:, s, :], pair[s][:], raw[:, s, :], ALU.add).then_inc(resid_done[s], 1)
                dve.wait_ge(out_root, b + 1)
                dve.reciprocal(rstd[:, bass.ds(b, 1)], rootms[:, bass.ds(b, 1)]).then_inc(out_rstd, 1)
                dve.wait_ge(out_rstd, b + 1)
                dve.wait_ge(fg_loaded, 16)
                dve.wait_ge(out_stored[s], i * 16)
                dve.scalar_tensor_tensor(out=tile[:, s, :], in0=raw[:, s, :], scalar=rstd[:, bass.ds(b, 1)],
                                         in1=side[:, 0, 0:D], op0=ALU.mult, op1=ALU.mult).then_inc(out_ready[s], 1)

            with dve.Fori(0, SB // 2 - 1) as i:
                for s in range(2):
                    merged_rest(i + 1, s)
                    finish(i, s)
            for s in range(2):
                finish(SB // 2 - 1, s)

        @block.tensor
        def _(pe):
            def step(slot, count, operand_hi, operand_lo, k_blocks=KB):
                pe.wait_ge(lo_done[slot], count + 1)
                for k in range(k_blocks):
                    at = slice(k * P, (k + 1) * P)
                    first, final = k == 0, k == k_blocks - 1
                    for b in range(2):
                        pe.matmul(pair[slot][:, half(b)], w_hi[:, slot, at], operand_hi[:, k, half(b)],
                                  start=first, stop=False)
                    for b in range(2):
                        pe.matmul(pair[slot][:, half(b)], w_hi[:, slot, at], operand_lo[:, k, half(b)],
                                  start=False, stop=False)
                    for b in range(2):
                        last = pe.matmul(pair[slot][:, half(b)], w_lo[:, slot, at], operand_hi[:, k, half(b)],
                                         start=False, stop=final)
                last.then_inc(step_done[slot], 1)

            pe.wait_ge(const_done, 2)
            pe.wait_ge(param_loaded, 16 * 8)
            for at, n in ((0, P), (P, TAPS_B * KB - P), (2 * P, PC_END - PC_CONV_A)):
                pe.transpose(pair[0][:, at:at + n], raw[0:n, 0, at:at + P], ident[0:n, 0:n]).then_inc(param_turned, 1)
            for g in range(2):
                pe.wait_ge(x_scaled, 4 * g + 4)
                for k in range(KB):
                    n = g * KB + k
                    if n >= 4:
                        pe.wait_ge(u_lo_done, n - 3)
                    for j in range(4):
                        turned = pe.transpose(misc[:, n % 4, j * P:(j + 1) * P],
                                              glu[:, 4 * g + j, PAD_B + k * P:PAD_B + (k + 1) * P], ident[:])
                    turned.then_inc(x_turned, 1)
            pe.wait_ge(param_copied, 2)
            pe.wait_ge(u_lo_done, 2 * KB)

            with pe.Fori(0, KB) as c:
                pe.wait_ge(glu_done, c)
                step(0, c + Q_B_IN, u_hi, u_lo)
                pe.wait_ge(gate_b_done, c)
                step(1, c + Q_B_IN, u_hi, u_lo)
            pe.wait_ge(glu_done, KB)
            pe.wait_ge(gate_b_done, KB)
            with pe.Fori(0, KB) as c:
                q = c * 2 + Q_A_IN
                pe.wait_ge(b_a_done, c)
                step(0, q, u_hi, u_lo)
                pe.wait_ge(z_a_done, c)
                step(1, q, u_hi, u_lo)
                pe.wait_ge(c_a_copied, c + 1)
                step(0, q + 1, u_hi, u_lo)
                pe.wait_ge(cx_done, c + 1)
                step(1, q + 1, u_hi, u_lo)

            def gate_out(branch, q, d):
                pe.wait_ge(gate_done[branch], d)
                step(0, d + q, u_hi, u_lo)
                pe.wait_ge(gated[branch], d)
                step(1, d + q, y_hi, y_lo)

            pe.wait_ge(b_a_done, KB)
            pe.wait_ge(y_a_lo, KB)
            with pe.Fori(0, 6) as d:
                gate_out("a", Q_A_OUT, d)

            def mean_of(source, target):
                for b in range(2):
                    last = pe.matmul(target[:, half(b)], ones[:], source[:, half(b)], start=True, stop=True)
                return last

            pe.wait_ge(fills, 4)
            pe.wait_ge(ln_sum, KB - 1)
            mean_of(side[:, 0, :], misc2[:, 0, :]).then_inc(mean_done, 1)
            for d in range(6, KB):
                gate_out("a", Q_A_OUT, d)

            pe.wait_ge(gate_done["a"], KB)
            step(0, Q_B_Z, u_hi, u_lo)
            pe.wait_ge(ln_sqsum, KB)
            mean_of(side[:, 1, :], misc2[:, 0, :]).then_inc(var_done, 1)
            pe.wait_ge(gated["a"], KB)
            step(1, Q_B_Z, u_hi, u_lo)
            with pe.Fori(1, KB // 2) as i:
                for s in range(2):
                    pe.wait_ge(z_b_done[s], i)
                    step(s, i + Q_B_Z, u_hi, u_lo)
            for s in range(2):
                pe.wait_ge(z_b_done[s], KB // 2)
            pe.wait_ge(y_b_lo, KB)
            with pe.Fori(0, 4) as d:
                gate_out("b", Q_B_OUT, d)
            pe.wait_ge(mem_scaled, MB)
            for k in range(KB):
                for b in range(MB):
                    turned = pe.transpose(score[:, k, b * P:(b + 1) * P], side[:, b, k * P:(k + 1) * P], ident[:])
            turned.then_inc(mem_turned, 1)
            with pe.Fori(4, KB) as d:
                gate_out("b", Q_B_OUT, d)

            pe.wait_ge(gate_done["b"], KB)
            pe.wait_ge(gated["b"], KB)
            pe.wait_ge(mem_lo_done, KB)
            with pe.Fori(0, HEADS) as h:
                q = h * 4 + Q_ATT

                def k_step(j):
                    pe.wait_ge(lo_done[0], q + j + 1)
                    for k in range(KB):
                        at = slice(k * P, (k + 1) * P)
                        pe.matmul(pair[0][:, 0:MEM], w_hi[:, 0, at], mem_hi[:, k, :], start=k == 0, stop=False)
                        pe.matmul(pair[0][:, 0:MEM], w_hi[:, 0, at], mem_lo[:, k, :], start=False, stop=False)
                        last = pe.matmul(pair[0][:, 0:MEM], w_lo[:, 0, at], mem_hi[:, k, :], start=False,
                                         stop=k == KB - 1)
                    last.then_inc(step_done[0], 1)

                def v_step(j):
                    pe.wait_ge(lo_done[0], q + j + 3)
                    for b in range(MB):
                        rows = slice(b * P, (b + 1) * P)
                        target = pair[0][:, b * HALF:b * HALF + P]
                        for k in range(KB):
                            at = slice(k * P, (k + 1) * P)
                            pe.matmul(target, mem_hi[:, k, rows], w_hi[:, 0, at], start=k == 0, stop=False)
                            pe.matmul(target, mem_hi[:, k, rows], w_lo[:, 0, at], start=False, stop=False)
                            last = pe.matmul(target, mem_lo[:, k, rows], w_hi[:, 0, at], start=False,
                                             stop=k == KB - 1)
                    last.then_inc(step_done[0], 1)

                pe.wait_ge(y_x_product, h * 2)
                k_step(0)
                step(1, q, u_hi, u_lo)
                pe.wait_ge(k_lo_done, h * 2 + 1)
                k_step(1)
                pe.wait_ge(q_lo_done, h * 2 + 1)
                step(1, q + 1, u_hi, u_lo)
                pe.wait_ge(k_lo_done, h * 2 + 2)
                v_step(0)
                pe.wait_ge(q_lo_done, h * 2 + 2)
                pe.wait_ge(pt_lo_done, h * MB)
                for b in range(SB):
                    rows = slice(b * P, (b + 1) * P)
                    for j in range(2):
                        q_at = KB - 2 + j
                        pe.matmul(score[:, b, :], y_hi[:, q_at, rows], k_hi[:, j, :], start=j == 0, stop=False)
                        pe.matmul(score[:, b, :], y_hi[:, q_at, rows], k_lo[:, j, :], start=False, stop=False)
                        last = pe.matmul(score[:, b, :], y_lo[:, q_at, rows], k_hi[:, j, :], start=False, stop=j == 1)
                last.then_inc(scores_done, 1)
                step(1, q + 2, u_hi, u_lo)
                pe.wait_ge(v_lo_done, h * 2 + 1)
                v_step(1)
                pe.wait_ge(prob_done, h * SB + SB)
                for m in range(MB):
                    for b in range(SB):
                        turned = pe.transpose(misc2[:, m, b * P:(b + 1) * P],
                                              prob[:, b // 4, b % 4, m * P:(m + 1) * P], ident[:])
                turned.then_inc(prob_turned, 1)
                pe.wait_ge(z_x_done, h * 2 + 1)
                step(1, q + 3, u_hi, u_lo)
                pe.wait_ge(pt_lo_done, h * MB + MB)
                pe.wait_ge(v_lo_done, h * 2 + 2)
                pe.wait_ge(z_x_done, h * 2 + 1)
                for j in range(2):
                    cols = slice(j * P, (j + 1) * P)
                    if j == 1:
                        pe.wait_ge(z_x_done, h * 2 + 2)
                    for m in range(MB):
                        p_at = KB - 2 + m
                        for stationary, moving, first, final in ((v_hi, y_hi, m == 0, False),
                                                                 (v_hi, y_lo, False, False),
                                                                 (v_lo, y_hi, False, m == MB - 1)):
                            for b in range(2):
                                last = pe.matmul(pair[j][:, half(b)], stationary[:, m, cols],
                                                 moving[:, p_at, half(b)], start=first, stop=final)
                    last.then_inc(pv_done, 1)

            pe.wait_ge(y_x_product, 2 * HEADS)
            with pe.Fori(0, KB // 2) as i:
                for s in range(2):
                    pe.wait_ge(gate_x_done[s], i)
                    step(s, i + Q_G_X, u_hi, u_lo)
            for s in range(2):
                pe.wait_ge(gate_x_done[s], KB // 2)
            pe.wait_ge(y_x_lo, 2 * HEADS)
            with pe.Fori(0, KB // 2) as i:
                for s in range(2):
                    pe.wait_ge(gated_x[s], i)
                    step(s, i + Q_X_OUT, y_hi, y_lo)
            for s in range(2):
                pe.wait_ge(gated_x[s], KB // 2)
            pe.wait_ge(wo_lo_done, KB)
            with pe.Fori(0, SB // 2) as i:
                for s in range(2):
                    pe.wait_ge(resid_done[s], i)
                    step(s, i + Q_FINAL, u_hi, u_lo)


_INS = ["x", "mem", "norm_g", "w_in", "conv_a_w", "w_out_a", "conv_b_w", "conv_b_b", "ln_b_g", "ln_b_b",
        "w_out_b", "mem_norm_g", "w_kv", "w_out_x", "w_o", "final_g"]


def kernel(**inputs):
    import concourse.bacc as bacc
    from concourse.bass_utils import run_bass_kernel_spmd

    nc = bacc.Bacc("TRN2", target_bir_lowering=False, num_devices=1)
    arrays, args = {}, []
    for name in _INS:
        a = np.ascontiguousarray(inputs[name])
        arrays[f"in_{name}"] = a
        args.append(nc.dram_tensor(f"in_{name}", a.shape, mybir.dt.from_np(a.dtype), kind="ExternalInput").ap())
    args.append(nc.dram_tensor("out", (1, S, D), F32, kind="ExternalOutput").ap())
    build(nc, *args)
    result = run_bass_kernel_spmd(nc, [arrays], core_ids=[0])
    return result.results[0]["out"]
```

```python
import numpy as np

import concourse.bass as bass
from concourse import mybir

P = 128
D = 1024
S = 1024
MEM = 256
KB = D // P
SB = S // P
MB = MEM // P
HALF = 512
HEADS = 4
HEAD_DIM = D // HEADS
TAPS_A = 3
TAPS_B = 31
PAD_A = TAPS_A - 1
PAD_B = TAPS_B - 1
EPS = 1e-6
SCALE = float(HEAD_DIM) ** -0.5

COL_B_A, COL_C_A, COL_X_A, COL_Z_A, COL_VAL_B, COL_GATE_B, COL_Z_B, COL_Q, COL_Z_X, COL_G_A, COL_G_B, COL_G_X = range(12)

Q_B_IN = 0
Q_A_IN = Q_B_IN + KB
Q_A_OUT = Q_A_IN + 2 * KB
Q_B_Z = Q_A_OUT + KB
Q_B_OUT = Q_B_Z + KB // 2
Q_ATT = Q_B_OUT + KB
Q_G_X = Q_ATT + 4 * HEADS
Q_X_OUT = Q_G_X + KB // 2
Q_FINAL = Q_X_OUT + KB // 2

PC_CONV_B = 0
PC_CONV_A = 256
PC_NORM_G = PC_CONV_A + TAPS_A * KB
PC_CONV_BIAS = PC_NORM_G + KB
PC_LN_G = PC_CONV_BIAS + KB
PC_LN_B = PC_LN_G + KB
PC_MEM_G = PC_LN_B + KB
PC_END = PC_MEM_G + KB

SQUARES_ACT = [0, 2, 3, 4, 6]
SQUARES_DVE = [1, 5, 7]

LN_AT = [[], [], [], [], [0, 1, 2], [3, 4, 5], [6, 7], []]

MEM_ORDER = list(range(0, KB, 2)) + list(range(1, KB, 2))

F32 = mybir.dt.float32
F32R = mybir.dt.float32r
ACT = mybir.ActivationFunctionType
ALU = mybir.AluOpType
AX = mybir.AxisListType


def build(nc, x, mem, norm_g, w_in, conv_a_w, w_out_a, conv_b_w, conv_b_b, ln_b_g, ln_b_b, w_out_b,
          mem_norm_g, w_kv, w_out_x, w_o, final_g, out):
    from contextlib import ExitStack

    ctx = ExitStack()
    with ctx:
        place = [(nc.sbuf_base + 31) // 32 * 32]

        def sbuf(name, shape, dtype, at=None):
            size = int(np.prod(shape[1:])) * 4
            offset = place[0] if at is None else at
            tensor = nc.alloc_sbuf_tensor_at(name, shape, dtype, offset=offset)
            if at is None:
                place[0] += (size + 31) // 32 * 32
            return tensor

        u_hi = sbuf("u_hi", [P, KB, S], F32R)
        u_lo = sbuf("u_lo", [P, KB, S], F32R)
        y_hi = sbuf("y_hi", [P, KB, S], F32R)
        y_lo = sbuf("y_lo", [P, KB, S], F32R)
        raw = sbuf("raw", [P, 2, S], F32)
        w_hi = sbuf("w_hi", [P, 2, S], F32R)
        w_lo = sbuf("w_lo", [P, 2, S], F32R)
        tile = sbuf("tile", [P, 2, S], F32)
        side = sbuf("side", [P, 2, S + 4], F32)
        shared = place[0]
        glu = sbuf("glu", [P, KB, PAD_B + S], F32)
        mem_hi = sbuf("mem_hi", [P, KB, MEM], F32R, at=shared)
        mem_lo = sbuf("mem_lo", [P, KB, MEM], F32R, at=shared + 8192)
        k_hi = sbuf("k_hi", [P, 2, MEM], F32R, at=shared + 16384)
        k_lo = sbuf("k_lo", [P, 2, MEM], F32R, at=shared + 18432)
        v_hi = sbuf("v_hi", [P, MB, HEAD_DIM], F32R, at=shared + 20480)
        v_lo = sbuf("v_lo", [P, MB, HEAD_DIM], F32R, at=shared + 22528)
        v_turned = sbuf("v_turned", [P, MEM], F32, at=shared + 24576)
        merged = sbuf("merged", [P, KB, S], F32, at=shared)
        spare = sbuf("spare", [P, S], F32)
        ident = sbuf("ident", [P, P], F32)
        ones = sbuf("ones", [P, P], F32)
        param = sbuf("param", [P, PC_END], F32)
        eps = sbuf("eps", [P, 1], F32)
        stat = sbuf("stat", [P, 56], F32)
        sumsq = stat[:, 0:8]
        rootms = stat[:, 8:16]
        rstd = stat[:, 16:24]
        peak = stat[:, 24:32]
        negpeak = stat[:, 32:40]
        rowsum = stat[:, 40:48]
        half_sumsq = stat[:, 48:49]
        half_meansq = stat[:, 49:50]
        assert place[0] <= nc.sbuf_usable_end, place[0]

        def half(b):
            return slice(b * HALF, (b + 1) * HALF)

        def psum(name):
            return ctx.enter_context(nc.psum_tensor(name, [P, S], F32))

        pair = [psum("pair0"), psum("pair1")]
        misc = ctx.enter_context(nc.psum_tensor("misc", [P, 4, HALF], F32))
        score = misc[:, :, :].rearrange("p b (s m) -> p (b s) m", m=MEM)
        misc2 = misc[:, :, :].rearrange("p (a b) f -> p a (b f)", a=2)
        prob = side[:, :, 0:S].rearrange("p a (s m) -> p a s m", m=MEM)

        part_a = nc.dram_tensor("part_a", (KB, P, S), F32).ap()
        part_ab = nc.dram_tensor("part_ab", (KB, P, S), F32).ap()

        def sem(name):
            return ctx.enter_context(nc.semaphore(name))

        def sem2(name):
            return [sem(name + "0"), sem(name + "1")]

        raw_loaded = sem2("raw_loaded")
        hi_done = sem2("hi_done")
        lo_done = sem2("lo_done")
        step_done = sem2("step_done")
        x_loaded = [sem(f"x_loaded{b}") for b in range(SB)]
        param_loaded = sem("param_loaded")
        const_done = sem("const_done")
        fills = sem("fills")
        param_turned = sem("param_turned")
        param_copied = sem("param_copied")
        sq_act_done = sem("sq_act_done")
        sq_dve_done = sem("sq_dve_done")
        root_done = sem("root_done")
        rstd_done = sem("rstd_done")
        x_scaled = sem("x_scaled")
        x_turned = sem("x_turned")
        u_hi_done = sem("u_hi_done")
        u_lo_done = sem("u_lo_done")
        gate_b_done = sem("gate_b_done")
        glu_done = sem("glu_done")
        conv_taps = sem("conv_taps")
        conv6_taps = sem("conv6_taps")
        ln_sum = sem("ln_sum")
        mean_done = sem("mean_done")
        ln_centered = sem("ln_centered")
        ln_squared = sem("ln_squared")
        ln_sqsum = sem("ln_sqsum")
        var_done = sem("var_done")
        ln_root = sem("ln_root")
        ln_rstd = sem("ln_rstd")
        ln_scaled = sem("ln_scaled")
        z_b_done = sem2("z_b_done")
        ln_swished = sem("ln_swished")
        y_b_product = sem("y_b_product")
        y_b_hi = sem("y_b_hi")
        y_b_lo = sem("y_b_lo")
        c_a_copied = sem("c_a_copied")
        cx_done = sem("cx_done")
        conv_a_done = sem("conv_a_done")
        b_a_done = sem("b_a_done")
        z_a_done = sem("z_a_done")
        y_a_product = sem("y_a_product")
        y_a_hi = sem("y_a_hi")
        y_a_lo = sem("y_a_lo")
        gate_done = {"a": sem("gate_a_done"), "b": sem("gate_b_out_done")}
        gated = {"a": sem("gated_a"), "b": sem("gated_b")}
        stored = {"a": sem2("stored_a"), "b": sem2("stored_ab")}
        part_a_loaded = sem("part_a_loaded")
        joined = sem("joined")
        mem_loaded = sem2("mem_loaded")
        mem_sq = sem("mem_sq")
        mem_root = sem("mem_root")
        mem_rstd = sem("mem_rstd")
        mem_scaled = sem("mem_scaled")
        mem_turned = sem("mem_turned")
        mem_hi_done = sem("mem_hi_done")
        mem_lo_done = sem("mem_lo_done")
        k_hi_done = sem("k_hi_done")
        k_lo_done = sem("k_lo_done")
        q_hi_done = sem("q_hi_done")
        q_lo_done = sem("q_lo_done")
        v_copied = sem("v_copied")
        v_turned_back = sem("v_turned_back")
        v_hi_done = sem("v_hi_done")
        v_lo_done = sem("v_lo_done")
        z_x_done = sem("z_x_done")
        scores_done = sem("scores_done")
        peak_done = sem("peak_done")
        negpeak_done = sem("negpeak_done")
        exp_done = sem("exp_done")
        denom_done = sem("denom_done")
        prob_done = sem("prob_done")
        prob_turned = sem("prob_turned")
        pt_hi_done = sem("pt_hi_done")
        pt_lo_done = sem("pt_lo_done")
        pv_done = sem("pv_done")
        y_x_product = sem("y_x_product")
        y_x_hi = sem("y_x_hi")
        y_x_lo = sem("y_x_lo")
        gate_x_done = sem2("gate_x_done")
        parts_loaded = sem2("parts_loaded")
        gated_x = sem2("gated_x")
        merged_done = sem2("merged_done")
        wo_loaded = sem2("wo_loaded")
        early_hi = sem("early_hi")
        early_lo = sem("early_lo")
        wo_hi_done = sem2("wo_hi_done")
        wo_lo_done = sem2("wo_lo_done")
        half_done = sem("half_done")
        half_resid = sem("half_resid")
        half_sq = sem("half_sq")
        half_mean = sem("half_mean")
        half_ready = sem("half_ready")
        xres_loaded = sem2("xres_loaded")
        fg_loaded = sem("fg_loaded")
        resid_done = sem2("resid_done")
        out_sq = sem("out_sq")
        out_root = sem("out_root")
        out_rstd = sem("out_rstd")
        out_ready = sem2("out_ready")
        out_stored = sem2("out_stored")

        w_in_t = w_in[0].rearrange("(k p) (g e) -> p k g e", p=P, e=P)
        w_kv_t = w_kv[0].rearrange("(k p) (g e) -> p k g e", p=P, e=P)
        w_out_t = {n: w[0].rearrange("(k p) (g e) -> p k g e", p=P, e=P)
                   for n, w in (("a", w_out_a), ("b", w_out_b), ("x", w_out_x))}
        w_o_rows = w_o[0].rearrange("(k p) e -> k p e", p=P)
        x_blocks = x[0].rearrange("(b p) d -> b p d", p=P)
        mem_blocks = mem[0].rearrange("(b p) d -> b p d", p=P)
        out_blocks = out[0].rearrange("(b p) d -> b p d", p=P)

        def wait(engine, semaphore, count):
            if not (isinstance(count, int) and count == 0):
                engine.wait_ge(semaphore, count)

        def peeled(engine, n, body, last=False):
            body(0)
            with engine.Fori(1, n - 1 if last else n) as i:
                body(i)
            if last:
                body(n - 1)

        block = ctx.enter_context(nc.Block())

        @block.sync
        def _(sp):
            def load(slot, count, source):
                wait(sp, lo_done[slot], count)
                sp.dma_start(raw[:, slot, :].rearrange("p (k e) -> p k e", e=P), source).then_inc(raw_loaded[slot], 16)

            def b_in(c):
                load(0, Q_B_IN + c, w_in_t[:, :, COL_GATE_B * KB + c, :])
                load(1, Q_B_IN + c, w_in_t[:, :, COL_VAL_B * KB + c, :])

            def load_x(b):
                sp.dma_start(glu[:, b, PAD_B:], x_blocks[b]).then_inc(x_loaded[b], 16)

            for b in range(SB // 2):
                load_x(b)
            conv_b_rows = conv_b_w[0].rearrange("j (k c) -> (j k) c", c=P)
            sp.dma_start(spare[:, 0:P], conv_b_rows[0:P]).then_inc(param_loaded, 16)
            sp.dma_start(spare[0:TAPS_B * KB - P, P:2 * P], conv_b_rows[P:TAPS_B * KB]).then_inc(param_loaded, 16)
            at = 0
            for source, n in ((conv_a_w[0].rearrange("j (k c) -> (j k) c", c=P), TAPS_A * KB),
                              (norm_g.rearrange("l (k c) -> (l k) c", c=P), KB),
                              (conv_b_b.rearrange("l (k c) -> (l k) c", c=P), KB),
                              (ln_b_g.rearrange("l (k c) -> (l k) c", c=P), KB),
                              (ln_b_b.rearrange("l (k c) -> (l k) c", c=P), KB),
                              (mem_norm_g.rearrange("l (k c) -> (l k) c", c=P), KB)):
                sp.dma_start(spare[at:at + n, 2 * P:3 * P], source).then_inc(param_loaded, 16)
                at += n
            load(0, Q_B_IN, w_in_t[:, :, COL_GATE_B * KB, :])
            for b in range(SB // 2, SB):
                load_x(b)
            load(1, Q_B_IN, w_in_t[:, :, COL_VAL_B * KB, :])
            with sp.Fori(1, KB) as c:
                b_in(c)
            with sp.Fori(0, KB) as c:
                load(0, Q_A_IN + c * 2, w_in_t[:, :, COL_C_A * KB + c, :])
                load(1, Q_A_IN + c * 2, w_in_t[:, :, COL_X_A * KB + c, :])
                load(0, Q_A_IN + c * 2 + 1, w_in_t[:, :, COL_B_A * KB + c, :])
                load(1, Q_A_IN + c * 2 + 1, w_in_t[:, :, COL_Z_A * KB + c, :])
            with sp.Fori(0, KB) as d:
                load(0, Q_A_OUT + d, w_in_t[:, :, COL_G_A * KB + d, :])
                load(1, Q_A_OUT + d, w_out_t["a"][:, :, d, :])
            with sp.Fori(0, KB // 2) as i:
                load(0, Q_B_Z + i, w_in_t[:, :, COL_Z_B * KB + i * 2, :])
                load(1, Q_B_Z + i, w_in_t[:, :, COL_Z_B * KB + i * 2 + 1, :])
            for s in range(2):
                sp.wait_ge(stored["a"][s], 16 * (KB // 2))

            def b_out(d):
                load(0, Q_B_OUT + d, w_in_t[:, :, COL_G_B * KB + d, :])
                load(1, Q_B_OUT + d, w_out_t["b"][:, :, d, :])
                wait(sp, joined, d)
                sp.dma_start(spare[:], part_a[d]).then_inc(part_a_loaded, 16)

            for d in range(2):
                b_out(d)
            for b in range(MB):
                sp.wait_ge(ln_scaled, KB)
                sp.dma_start(side[:, b, 0:D], mem_blocks[b]).then_inc(mem_loaded[b], 16)
            with sp.Fori(2, KB) as d:
                b_out(d)
            with sp.Fori(0, HEADS) as h:
                q = Q_ATT + h * 4
                load(0, q, w_kv_t[:, :, h * 2, :])
                load(1, q, w_in_t[:, :, COL_Q * KB + h * 2, :])
                load(0, q + 1, w_kv_t[:, :, h * 2 + 1, :])
                load(1, q + 1, w_in_t[:, :, COL_Q * KB + h * 2 + 1, :])
                load(0, q + 2, w_kv_t[:, :, KB + h * 2, :])
                load(1, q + 2, w_in_t[:, :, COL_Z_X * KB + h * 2, :])
                load(0, q + 3, w_kv_t[:, :, KB + h * 2 + 1, :])
                load(1, q + 3, w_in_t[:, :, COL_Z_X * KB + h * 2 + 1, :])
            with sp.Fori(0, KB // 2) as i:
                load(0, Q_G_X + i, w_in_t[:, :, COL_G_X * KB + i * 2, :])
                load(1, Q_G_X + i, w_in_t[:, :, COL_G_X * KB + i * 2 + 1, :])
            sp.wait_ge(joined, KB)
            sp.dma_start(spare[:], final_g.rearrange("(a d) -> a d", a=1).to_broadcast([P, D])).then_inc(fg_loaded, 16)
            sp.wait_ge(y_x_lo, 2 * HEADS)
            sp.wait_ge(prob_turned, HEADS)

            def x_out(i):
                for s in range(2):
                    d = i * 2 + s
                    load(s, i + Q_X_OUT, w_out_t["x"][:, :, d, :])
                    wait(sp, merged_done[s], i)
                    sp.dma_start(tile[:, s, :], part_ab[d]).then_inc(parts_loaded[s], 16)
                    wait(sp, wo_lo_done[s], i)
                    sp.dma_start(side[:, s, 0:S], w_o_rows[d]).then_inc(wo_loaded[s], 16)

            peeled(sp, KB // 2, x_out)

            def residual(i):
                for s in range(2):
                    if isinstance(i, int):
                        sp.wait_ge(lo_done[s], Q_FINAL)
                    wait(sp, out_ready[s], i)
                    sp.dma_start(raw[:, s, :], x_blocks[i * 2 + s]).then_inc(xres_loaded[s], 16)

            peeled(sp, SB // 2, residual)
            sp.wait_ge(out_ready[1], SB // 2)
            sp.dma_start(out_blocks[SB - 1][:, half(1)], tile[:, 1, half(1)]).then_inc(out_stored[1], 16)
            sp.wait_ge(out_stored[0], 16 * (SB // 2))
            sp.wait_ge(out_stored[1], 16 * (SB // 2 + 1))

        @block.gpsimd
        def _(pool):
            nc.gpsimd.memset(ident[:], 0.0).then_inc(const_done, 1)
            pool.wait_ge(const_done, 1)
            nc.gpsimd.affine_select(out=ident[:], in_=ident[:], compare_op=ALU.not_equal, fill=1.0, base=0,
                                    pattern=[[-1, P]], channel_multiplier=1).then_inc(const_done, 1)

        @block.scalar
        def _(act):
            def w_round(slot, count):
                act.wait_ge(raw_loaded[slot], count * 16 + 16)
                wait(act, step_done[slot], count)
                act.activation(w_hi[:, slot, :], raw[:, slot, :], ACT.Copy).then_inc(hi_done[slot], 1)

            def square(b):
                act.wait_ge(x_loaded[b], 16)
                wait(act, sq_act_done, SQUARES_ACT.index(b))
                act.activation(tile[:, 0, :], glu[:, b, PAD_B:], ACT.Square,
                               accum_out=sumsq[:, b:b + 1]).then_inc(sq_act_done, 1)

            def root(b):
                if b in SQUARES_ACT:
                    act.wait_ge(sq_act_done, SQUARES_ACT.index(b) + 1)
                else:
                    act.wait_ge(sq_dve_done, SQUARES_DVE.index(b) + 1)
                act.activation(rootms[:, b:b + 1], sumsq[:, b:b + 1], ACT.Sqrt,
                               scale=1.0 / D, bias=eps[:, 0:1]).then_inc(root_done, 1)

            def u_round(g, k):
                n = g * KB + k
                act.wait_ge(x_turned, n + 1)
                act.activation(u_hi[:, k, half(g)], misc[:, n % 4, :], ACT.Copy,
                               scale=param[:, PC_NORM_G + k:PC_NORM_G + k + 1]).then_inc(u_hi_done, 1)

            act.wait_ge(fills, 1)
            act.activation(rootms[:, 0:1], eps[:, 0:1], ACT.Sqrt).then_inc(root_done, 1)
            square(0)
            act.wait_ge(root_done, 1)
            root(0)
            root(1)
            square(2)
            root(2)
            square(3)
            root(3)
            w_round(0, 0)
            act.wait_ge(param_copied, 2)
            for k in range(KB):
                u_round(0, k)
                if k == 2:
                    square(4)
                    root(4)
                if k == 4:
                    root(5)
                if k == 5:
                    square(6)
                    root(6)
            root(7)
            w_round(1, 0)
            for k in range(KB):
                u_round(1, k)

            def b_in(c):
                w_round(0, Q_B_IN + c + 1)
                wait(act, glu_done, c)
                act.activation(tile[:, 0, :], pair[0][:], ACT.Sigmoid).then_inc(gate_b_done, 1)
                w_round(1, Q_B_IN + c + 1)

            peeled(act, KB, b_in)

            act.wait_ge(conv_taps, 2 * TAPS_B)
            act.wait_ge(glu_done, KB)

            def a_in(c):
                q = Q_A_IN + c * 2
                w_round(0, q + 1)
                wait(act, y_a_product, c)
                act.activation(tile[:, 0, :], pair[0][:], ACT.Copy).then_inc(c_a_copied, 1)
                w_round(1, q + 1)
                w_round(0, q + 2)
                w_round(1, q + 2)
                wait(act, y_a_lo, c)
                act.activation(tile[:, 1, :], pair[1][:], ACT.Silu).then_inc(z_a_done, 1)
                act.wait_ge(y_a_product, c + 1)
                act.activation(y_hi[:, c, :], tile[:, 1, :], ACT.Copy).then_inc(y_a_hi, 1)

            peeled(act, KB, a_in)

            def gate_out(branch, q, i, s):
                d = i * 2 + s
                part = part_a if branch == "a" else part_ab
                w_round(0, q + d + 1)
                wait(act, stored[branch][s], i * 16)
                act.activation(tile[:, s, :], pair[0][:], ACT.Sigmoid).then_inc(gate_done[branch], 1)
                w_round(1, q + d + 1)
                act.wait_ge(gated["a"] if branch == "a" else joined, d + 1)
                act.dma_start(part[d], tile[:, s, :]).then_inc(stored[branch][s], 16)

            act.wait_ge(y_a_lo, KB)
            for i in range(KB // 2):
                for s in range(2):
                    gate_out("a", Q_A_OUT, i, s)
                    for c in LN_AT[i * 2 + s]:
                        act.wait_ge(ln_centered, c + 1)
                        wait(act, ln_sqsum, c)
                        act.activation(misc2[:, 1, :], glu[:, c, PAD_B:], ACT.Square).then_inc(ln_squared, 1)

            act.wait_ge(var_done, 1)
            act.activation(side[:, 0, 0:S], misc2[:, 0, :], ACT.Sqrt, bias=eps[:, 0:1]).then_inc(ln_root, 1)
            act.wait_ge(stored["a"][0], 64)
            act.wait_ge(stored["a"][1], 64)

            def z_b(i, s):
                c = i * 2 + s
                act.wait_ge(step_done[s], Q_B_Z + i + 1)
                if s == 0:
                    wait(act, y_b_lo, i * 2)
                act.activation(tile[:, s, :], pair[s][:], ACT.Silu).then_inc(z_b_done[s], 1)
                act.wait_ge(ln_scaled, c + 1)
                act.activation(glu[:, c, PAD_B:], glu[:, c, PAD_B:], ACT.Silu,
                               scale=param[:, bass.ds(c + PC_LN_G, 1)],
                               bias=param[:, bass.ds(c + PC_LN_B, 1)]).then_inc(ln_swished, 1)
                act.wait_ge(y_b_product, c + 1)
                act.activation(y_hi[:, c, :], tile[:, s, :], ACT.Copy).then_inc(y_b_hi, 1)

            def z_b_pair(i):
                w_round(0, Q_B_Z + i + 1)
                z_b(i, 0)
                w_round(1, Q_B_Z + i + 1)
                z_b(i, 1)

            peeled(act, KB // 2, z_b_pair)

            act.wait_ge(y_b_lo, KB)
            for s in range(2):
                gate_out("b", Q_B_OUT, 0, s)
            for b in range(MB):
                act.wait_ge(mem_loaded[b], 16)
                act.activation(misc2[:, b, :], side[:, b, 0:D], ACT.Square,
                               accum_out=sumsq[:, b:b + 1]).then_inc(mem_sq, 1)
            act.wait_ge(mem_sq, MB)
            act.activation(rootms[:, 0:MB], sumsq[:, 0:MB], ACT.Sqrt, scale=1.0 / D,
                           bias=eps[:, 0:1]).then_inc(mem_root, 1)
            for s in range(2):
                gate_out("b", Q_B_OUT, 1, s)
            act.wait_ge(mem_turned, 1)
            for n, k in enumerate(MEM_ORDER):
                if n >= 4:
                    act.wait_ge(mem_lo_done, n - 3)
                act.activation(mem_hi[:, k, :], score[:, k, :], ACT.Copy,
                               scale=param[:, PC_MEM_G + k:PC_MEM_G + k + 1]).then_inc(mem_hi_done, 1)
            with act.Fori(2, 4) as i:
                for s in range(2):
                    gate_out("b", Q_B_OUT, i, s)

            act.wait_ge(stored["b"][0], 64)
            act.wait_ge(stored["b"][1], 64)

            def y_round(h):
                act.wait_ge(y_x_product, h * 2 + 2)
                for j in range(2):
                    act.activation(y_hi[:, h * 2 + j, :], tile[:, j, :], ACT.Copy).then_inc(y_x_hi, 1)

            def head(h):
                q = Q_ATT + h * 4

                def k_round(j):
                    w_round(0, q + j + 1)
                    act.activation(k_hi[:, j, :], pair[0][:, 0:MEM], ACT.Copy).then_inc(k_hi_done, 1)

                def q_round(j):
                    w_round(1, q + j + 1)
                    act.activation(y_hi[:, KB - 2 + j, :], pair[1][:], ACT.Copy).then_inc(q_hi_done, 1)

                def v_copy(j):
                    w_round(0, q + j + 3)
                    act.activation(v_turned[:], pair[0][:, 0:MEM], ACT.Copy).then_inc(v_copied, 1)

                def v_round(j):
                    act.wait_ge(v_turned_back, h * 2 + j + 1)
                    act.activation(v_hi[:, :, j * P:(j + 1) * P],
                                   pair[0][:, HALF:HALF + MEM].rearrange("p (b f) -> p b f", b=2),
                                   ACT.Copy).then_inc(v_hi_done, 1)

                def z_x(j):
                    w_round(1, q + j + 3)
                    wait(act, y_x_lo, h * 2)
                    act.activation(tile[:, j, :], pair[1][:], ACT.Silu).then_inc(z_x_done, 1)

                k_round(0)
                q_round(0)
                k_round(1)
                q_round(1)
                v_copy(0)
                if not (isinstance(h, int) and h == 0):
                    y_round(h - 1)
                act.wait_ge(negpeak_done, h + 1)
                for b in range(SB):
                    act.activation(prob[:, b // 4, b % 4, :], score[:, b, :], ACT.Exp, scale=SCALE,
                                   bias=negpeak[:, b:b + 1], accum_out=rowsum[:, b:b + 1]).then_inc(exp_done, 1)
                v_round(0)
                z_x(0)
                v_copy(1)
                for b in range(MB):
                    act.wait_ge(prob_turned, h + 1)
                    act.activation(y_hi[:, h * 2 + b, :], misc2[:, b, :], ACT.Copy).then_inc(pt_hi_done, 1)
                v_round(1)
                z_x(1)

            peeled(act, HEADS, head)
            y_round(HEADS - 1)

            with act.Fori(0, KB // 2) as i:
                for s in range(2):
                    w_round(s, i + (Q_G_X + 1))
                    act.activation(merged[:, i * 2 + s, :], pair[s][:], ACT.Sigmoid).then_inc(gate_x_done[s], 1)

            def wo_round(i, s):
                act.wait_ge(wo_loaded[s], i * 16 + 16)
                act.wait_ge(step_done[1], Q_X_OUT)
                act.activation(u_hi[:, i * 2 + s, :], side[:, s, 0:S], ACT.Copy).then_inc(wo_hi_done[s], 1)

            with act.Fori(0, KB // 2 - 1) as i:
                for s in range(2):
                    wo_round(i, s)
                    w_round(s, i + (Q_X_OUT + 1))
            for s in range(2):
                wo_round(KB // 2 - 1, s)

            def merged_round(i, s, k=slice(0, KB), done=hi_done):
                act.activation(w_hi[:, s, :].rearrange("p (k e) -> p k e", e=P)[:, k, :],
                               merged[:, k, bass.ds((i * 2 + s) * P, P)], ACT.Copy).then_inc(done[s], 1)

            act.wait_ge(step_done[0], Q_FINAL)
            act.wait_ge(merged_done[0], KB // 2)
            act.wait_ge(merged_done[1], KB // 2 - 1)
            merged_round(0, 0, slice(0, KB - 1), [early_hi])
            act.wait_ge(merged_done[1], KB // 2)
            merged_round(0, 0, slice(KB - 1, KB))
            act.wait_ge(step_done[1], Q_FINAL)
            merged_round(0, 1)

            def finish(i, s):
                b = i * 2 + s
                act.wait_ge(resid_done[s], i + 1)
                act.activation(misc2[:, s, :], raw[:, s, :], ACT.Square,
                               accum_out=sumsq[:, bass.ds(b, 1)]).then_inc(out_sq, 1)
                act.wait_ge(out_sq, b + 1)
                act.activation(rootms[:, bass.ds(b, 1)], sumsq[:, bass.ds(b, 1)], ACT.Sqrt, scale=1.0 / D,
                               bias=eps[:, 0:1]).then_inc(out_root, 1)
                act.wait_ge(out_ready[s], i + 1)
                act.dma_start(out_blocks[b], tile[:, s, :]).then_inc(out_stored[s], 16)

            with act.Fori(0, SB // 2 - 1) as i:
                for s in range(2):
                    act.wait_ge(step_done[s], i + (Q_FINAL + 1))
                    merged_round(i + 1, s)
                    finish(i, s)
            finish(SB // 2 - 1, 0)
            act.wait_ge(half_resid, 1)
            act.activation(misc2[:, 1, half(0)], raw[:, 1, half(0)], ACT.Square, accum_out=half_sumsq).then_inc(half_sq, 1)
            act.wait_ge(resid_done[1], SB // 2)
            act.activation(misc2[:, 1, half(1)], raw[:, 1, half(1)], ACT.Square,
                           accum_out=sumsq[:, SB - 1:SB]).then_inc(out_sq, 1)
            act.wait_ge(out_sq, SB)
            act.wait_ge(half_mean, 1)
            act.activation(rootms[:, SB - 1:SB], sumsq[:, SB - 1:SB], ACT.Sqrt, scale=1.0 / D,
                           bias=half_meansq).then_inc(out_root, 1)
            act.wait_ge(half_ready, 1)
            act.dma_start(out_blocks[SB - 1][:, half(0)], tile[:, 1, half(0)]).then_inc(out_stored[1], 16)

        @block.vector
        def _(dve):
            def w_rest(slot, count):
                dve.wait_ge(hi_done[slot], count + 1)
                dve.tensor_tensor(w_lo[:, slot, :], raw[:, slot, :], w_hi[:, slot, :].bitcast(F32),
                                  ALU.subtract).then_inc(lo_done[slot], 1)

            dve.memset(eps[:], EPS).then_inc(fills, 1)
            dve.memset(ones[:], 1.0 / D).then_inc(fills, 1)
            dve.memset(glu[:, :, 0:PAD_B], 0.0).then_inc(fills, 1)
            dve.memset(side[:, 1, 0:PAD_A], 0.0).then_inc(fills, 1)

            def square(b):
                dve.wait_ge(x_loaded[b], 16)
                wait(dve, sq_dve_done, SQUARES_DVE.index(b))
                dve.tensor_tensor_reduce(tile[:, 1, :], glu[:, b, PAD_B:], glu[:, b, PAD_B:], 1.0, 0.0,
                                         ALU.mult, ALU.add, sumsq[:, b:b + 1]).then_inc(sq_dve_done, 1)

            def scale_x(b):
                dve.wait_ge(root_done, b + 2)
                dve.reciprocal(rstd[:, b:b + 1], rootms[:, b:b + 1]).then_inc(rstd_done, 1)
                dve.wait_ge(rstd_done, b + 1)
                dve.tensor_scalar(glu[:, b, PAD_B:], glu[:, b, PAD_B:], rstd[:, b:b + 1], None,
                                  ALU.mult).then_inc(x_scaled, 1)

            def u_rest(g, k):
                n = g * KB + k
                dve.wait_ge(u_hi_done, n + 1)
                dve.scalar_tensor_tensor(out=u_lo[:, k, half(g)], in0=misc[:, n % 4, :],
                                         scalar=param[:, PC_NORM_G + k:PC_NORM_G + k + 1],
                                         in1=u_hi[:, k, half(g)].bitcast(F32), op0=ALU.mult,
                                         op1=ALU.subtract).then_inc(u_lo_done, 1)

            square(1)
            scale_x(0)
            scale_x(1)
            scale_x(2)
            scale_x(3)
            dve.wait_ge(param_turned, 3)
            dve.tensor_copy(param[:, 0:TAPS_B * KB], pair[0][:, 0:TAPS_B * KB]).then_inc(param_copied, 1)
            dve.tensor_copy(param[:, PC_CONV_A:PC_END], pair[0][:, PC_CONV_A:PC_END]).then_inc(param_copied, 1)
            dve.wait_ge(param_copied, 2)
            w_rest(0, 0)
            for k in range(KB):
                u_rest(0, k)
                if k == 2:
                    square(5)
                if k == 3:
                    scale_x(4)
                if k == 4:
                    scale_x(5)
                if k == 5:
                    square(7)
                if k == 6:
                    scale_x(6)
            scale_x(7)
            w_rest(1, 0)
            for k in range(KB):
                u_rest(1, k)
            dve.wait_ge(fills, 4)

            def conv_tap(c, tap, sums, done, source=None, counted=conv_taps):
                wait(dve, counted, done)
                weight = param[:, bass.ds(tap * KB + c + PC_CONV_B, 1)]
                if source is not None:
                    dve.scalar_tensor_tensor(out=sums, in0=source, scalar=weight, in1=sums, op0=ALU.mult,
                                             op1=ALU.add).then_inc(counted, 1)
                elif tap == 0:
                    dve.tensor_scalar(sums, glu[:, c, 0:S], weight, param[:, bass.ds(c + PC_CONV_BIAS, 1)],
                                      ALU.mult, ALU.add).then_inc(counted, 1)
                elif tap < TAPS_B - 1:
                    dve.scalar_tensor_tensor(out=sums, in0=glu[:, c, tap:tap + S], scalar=weight, in1=sums,
                                             op0=ALU.mult, op1=ALU.add).then_inc(counted, 1)
                else:
                    dve.scalar_tensor_tensor(out=glu[:, c, PAD_B:], in0=glu[:, c, PAD_B:], scalar=weight,
                                             in1=sums, op0=ALU.mult, op1=ALU.add).then_inc(counted, 1)

            def two_convs(c, taps, sums, base):
                for tap in taps:
                    for s in range(2):
                        conv_tap(c + s, tap, sums[s], base + max(2 * tap + s - 1, 0))

            def two_convs_at(c, first, n, sums, done):
                for t in range(n):
                    for s in range(2):
                        conv_tap(c + s, first + t, sums[s], done + (2 * t + s),
                                 source=glu[:, c + s, bass.ds(first + t, S)])

            def b_in(c, taps=lambda part: None):
                w_rest(0, c + (Q_B_IN + 1))
                taps(0)
                w_rest(1, c + (Q_B_IN + 1))
                dve.wait_ge(gate_b_done, c + 1)
                dve.wait_ge(step_done[1], c + (Q_B_IN + 1))
                dve.tensor_tensor(glu[:, c, PAD_B:], pair[1][:], tile[:, 0, :], ALU.mult).then_inc(glu_done, 1)
                taps(1)

            sums_b_in = [side[:, 0, 0:S], tile[:, 1, :]]
            b_in(0)
            b_in(1)
            dve.wait_ge(glu_done, 2)
            two_convs(0, [0], sums_b_in, 0)
            with dve.Fori(0, 5) as i:
                b_in(i + 2, lambda part: two_convs_at(0, i * 5 + (3 * part + 1), 3 - part, sums_b_in,
                                                      i * 10 + (6 * part + 1)))
            b_in(7, lambda part: two_convs(0, range(26 + 3 * part, 29 + 2 * part), sums_b_in, 0))

            taps_before = 2 * TAPS_B
            dve.wait_ge(glu_done, KB)
            conv_tap(6, 0, spare[:], 0, counted=conv6_taps)

            def a_in(i):
                for s in range(2):
                    c = i * 2 + s
                    q = c * 2 + Q_A_IN

                    def taps(part):
                        for t in range(4):
                            tap = 16 * s + 4 * part + t
                            if tap < TAPS_B:
                                conv_tap(i + 2, tap, side[:, 0, 0:S], i * TAPS_B + (taps_before + tap))
                            if t == 1 and not (isinstance(c, int) and c == KB - 1):
                                tap = c * 4 + (part + 1)
                                conv_tap(6, tap, spare[:], tap, source=glu[:, 6, bass.ds(tap, S)],
                                         counted=conv6_taps)
                            elif t == 1 and part < 2:
                                conv_tap(6, 29 + part, spare[:], 29 + part, counted=conv6_taps)

                    w_rest(0, q + 1)
                    taps(0)
                    w_rest(1, q + 1)
                    dve.wait_ge(step_done[1], q + 1)
                    dve.wait_ge(c_a_copied, c + 1)
                    wait(dve, conv_a_done, c * TAPS_A)
                    dve.tensor_tensor(side[:, 1, PAD_A:PAD_A + S], pair[1][:], tile[:, 0, :],
                                      ALU.mult).then_inc(cx_done, 1)
                    dve.wait_ge(cx_done, c + 1)
                    for tap in range(TAPS_A):
                        weight = param[:, bass.ds(c + (PC_CONV_A + tap * KB), 1)]
                        wait(dve, conv_a_done, c * TAPS_A + tap)
                        if tap == 0:
                            dve.tensor_scalar(tile[:, 0, :], side[:, 1, 0:S], weight, None,
                                              ALU.mult).then_inc(conv_a_done, 1)
                        else:
                            dve.scalar_tensor_tensor(out=tile[:, 0, :], in0=side[:, 1, tap:tap + S],
                                                     scalar=weight, in1=tile[:, 0, :], op0=ALU.mult,
                                                     op1=ALU.add).then_inc(conv_a_done, 1)
                    taps(1)
                    w_rest(0, q + 2)
                    dve.wait_ge(step_done[0], q + 2)
                    dve.wait_ge(conv_a_done, c * TAPS_A + TAPS_A)
                    dve.tensor_tensor(tile[:, 0, :], pair[0][:], tile[:, 0, :], ALU.mult).then_inc(b_a_done, 1)
                    taps(2)
                    w_rest(1, q + 2)
                    dve.wait_ge(z_a_done, c + 1)
                    dve.wait_ge(b_a_done, c + 1)
                    dve.tensor_tensor(tile[:, 1, :], tile[:, 1, :], tile[:, 0, :], ALU.mult).then_inc(y_a_product, 1)
                    taps(3)
                    dve.wait_ge(y_a_hi, c + 1)
                    dve.tensor_tensor(y_lo[:, c, :], tile[:, 1, :], y_hi[:, c, :].bitcast(F32),
                                      ALU.subtract).then_inc(y_a_lo, 1)

            peeled(dve, KB // 2, a_in, last=True)

            def gate_out(branch, q, d, s, taps=lambda part: None):
                w_rest(0, d + (q + 1))
                taps(0)
                dve.wait_ge(step_done[1], d + (q + 1))
                dve.wait_ge(gate_done[branch], d + 1)
                dve.tensor_tensor(tile[:, s, :], pair[1][:], tile[:, s, :], ALU.mult).then_inc(gated[branch], 1)
                w_rest(1, d + (q + 1))
                taps(1)
                if branch == "b":
                    dve.wait_ge(gated[branch], d + 1)
                    dve.wait_ge(part_a_loaded, d * 16 + 16)
                    dve.tensor_tensor(tile[:, s, :], tile[:, s, :], spare[:], ALU.add).then_inc(joined, 1)

            taps_before = 6 * TAPS_B

            def last_conv(taps):
                for tap in taps:
                    conv_tap(KB - 1, tap, side[:, 0, 0:S], taps_before + tap)

            def add_square(c):
                dve.wait_ge(ln_squared, c + 1)
                if c == 0:
                    dve.tensor_copy(side[:, 1, 0:S], misc2[:, 1, :]).then_inc(ln_sqsum, 1)
                else:
                    dve.wait_ge(ln_sqsum, c)
                    dve.tensor_tensor(side[:, 1, 0:S], misc2[:, 1, :], side[:, 1, 0:S], ALU.add).then_inc(ln_sqsum, 1)

            for d in range(KB):
                gate_out("a", Q_A_OUT, d, d % 2,
                         lambda part: last_conv(range(11 * d + 6 * part, min(11 * d + 6 + 5 * part, TAPS_B))))
                if d == 3:
                    dve.wait_ge(conv_taps, (KB - 1) * TAPS_B)
                    dve.wait_ge(conv6_taps, TAPS_B)
                    dve.tensor_tensor(side[:, 0, 0:S], glu[:, 0, PAD_B:], glu[:, 1, PAD_B:],
                                      ALU.add).then_inc(ln_sum, 1)
                    for c in range(2, KB):
                        dve.wait_ge(ln_sum, c - 1)
                        dve.tensor_tensor(side[:, 0, 0:S], side[:, 0, 0:S], glu[:, c, PAD_B:],
                                          ALU.add).then_inc(ln_sum, 1)
                if LN_AT[d]:
                    dve.wait_ge(mean_done, 1)
                for c in LN_AT[d]:
                    dve.tensor_tensor(glu[:, c, PAD_B:], misc2[:, 0, :], glu[:, c, PAD_B:],
                                      ALU.subtract).then_inc(ln_centered, 1)
                    if c:
                        add_square(c - 1)
            add_square(KB - 1)

            dve.wait_ge(ln_root, 1)
            dve.reciprocal(side[:, 1, 0:S], side[:, 0, 0:S]).then_inc(ln_rstd, 1)
            dve.wait_ge(ln_rstd, 1)

            def ln_scale(c):
                dve.scalar_tensor_tensor(out=glu[:, c, PAD_B:], in0=glu[:, c, PAD_B:], scalar=-1.0,
                                         in1=side[:, 1, 0:S], op0=ALU.mult, op1=ALU.mult).then_inc(ln_scaled, 1)

            def z_b(c, i, s, last=False):
                dve.wait_ge(z_b_done[s], i + 1)
                dve.wait_ge(ln_swished, c + 1)
                dve.tensor_tensor(tile[:, s, :], tile[:, s, :], glu[:, c, PAD_B:], ALU.mult).then_inc(y_b_product, 1)
                if not last:
                    ln_scale(c + 1)
                dve.wait_ge(y_b_hi, c + 1)
                dve.tensor_tensor(y_lo[:, c, :], tile[:, s, :], y_hi[:, c, :].bitcast(F32),
                                  ALU.subtract).then_inc(y_b_lo, 1)

            ln_scale(0)
            for s in range(2):
                w_rest(s, Q_B_Z + 1)
                z_b(s, 0, s)
            with dve.Fori(1, KB // 2 - 1) as i:
                for s in range(2):
                    w_rest(s, i + (Q_B_Z + 1))
                    z_b(i * 2 + s, i, s)
            for s in range(2):
                w_rest(s, Q_B_Z + KB // 2)
                z_b(KB - 2 + s, KB // 2 - 1, s, last=(s == 1))

            for s in range(2):
                gate_out("b", Q_B_OUT, s, s)
            dve.wait_ge(mem_root, 1)
            dve.reciprocal(rstd[:, 0:MB], rootms[:, 0:MB]).then_inc(mem_rstd, 1)
            dve.wait_ge(mem_rstd, 1)
            for b in range(MB):
                dve.tensor_scalar(side[:, b, 0:D], side[:, b, 0:D], rstd[:, b:b + 1], None,
                                  ALU.mult).then_inc(mem_scaled, 1)
            for s in range(2):
                gate_out("b", Q_B_OUT, 2 + s, s)
            for n, k in enumerate(MEM_ORDER):
                dve.wait_ge(mem_hi_done, n + 1)
                dve.scalar_tensor_tensor(out=mem_lo[:, k, :], in0=score[:, k, :],
                                         scalar=param[:, PC_MEM_G + k:PC_MEM_G + k + 1],
                                         in1=mem_hi[:, k, :].bitcast(F32), op0=ALU.mult,
                                         op1=ALU.subtract).then_inc(mem_lo_done, 1)
            with dve.Fori(2, 4) as i:
                for s in range(2):
                    gate_out("b", Q_B_OUT, i * 2 + s, s)

            def y_product(h, j):
                dve.wait_ge(pv_done, h * 2 + j + 1)
                dve.wait_ge(z_x_done, h * 2 + j + 1)
                dve.tensor_tensor(tile[:, j, :], misc2[:, j, :], tile[:, j, :], ALU.mult).then_inc(y_x_product, 1)

            def y_rest(h):
                for j in range(2):
                    dve.wait_ge(y_x_hi, h * 2 + j + 1)
                    dve.tensor_tensor(y_lo[:, h * 2 + j, :], tile[:, j, :], y_hi[:, h * 2 + j, :].bitcast(F32),
                                      ALU.subtract).then_inc(y_x_lo, 1)

            def head(h):
                q = h * 4 + Q_ATT
                first_head = isinstance(h, int) and h == 0

                def k_rest(j):
                    w_rest(0, q + j + 1)
                    dve.wait_ge(k_hi_done, h * 2 + j + 1)
                    dve.tensor_tensor(k_lo[:, j, :], pair[0][:, 0:MEM], k_hi[:, j, :].bitcast(F32),
                                      ALU.subtract).then_inc(k_lo_done, 1)

                def q_rest(j):
                    w_rest(1, q + j + 1)
                    dve.wait_ge(q_hi_done, h * 2 + j + 1)
                    dve.tensor_tensor(y_lo[:, KB - 2 + j, :], pair[1][:], y_hi[:, KB - 2 + j, :].bitcast(F32),
                                      ALU.subtract).then_inc(q_lo_done, 1)

                def v_rest(j):
                    dve.wait_ge(v_hi_done, h * 2 + j + 1)
                    dve.tensor_tensor(v_lo[:, :, j * P:(j + 1) * P],
                                      pair[0][:, HALF:HALF + MEM].rearrange("p (b f) -> p b f", b=2),
                                      v_hi[:, :, j * P:(j + 1) * P].bitcast(F32),
                                      ALU.subtract).then_inc(v_lo_done, 1)

                k_rest(0)
                q_rest(0)
                k_rest(1)
                if not first_head:
                    y_product(h - 1, 0)
                q_rest(1)
                w_rest(0, q + 3)
                if not first_head:
                    y_product(h - 1, 1)
                dve.wait_ge(scores_done, h + 1)
                dve.tensor_reduce(peak, score[:, :, :], AX.X, ALU.max).then_inc(peak_done, 1)
                dve.wait_ge(peak_done, h + 1)
                dve.tensor_scalar(negpeak, peak, -SCALE, None, ALU.mult).then_inc(negpeak_done, 1)
                if not first_head:
                    y_rest(h - 1)
                v_rest(0)
                dve.wait_ge(exp_done, h * SB + SB)
                dve.reciprocal(rstd[:, 0:SB], rowsum).then_inc(denom_done, 1)
                dve.wait_ge(denom_done, h + 1)
                for b in range(SB):
                    dve.tensor_scalar(prob[:, b // 4, b % 4, :], prob[:, b // 4, b % 4, :], rstd[:, b:b + 1],
                                      None, ALU.mult).then_inc(prob_done, 1)
                w_rest(1, q + 3)
                w_rest(0, q + 4)
                for b in range(MB):
                    dve.wait_ge(pt_hi_done, h * MB + b + 1)
                    dve.tensor_tensor(y_lo[:, h * 2 + b, :], misc2[:, b, :], y_hi[:, h * 2 + b, :].bitcast(F32),
                                      ALU.subtract).then_inc(pt_lo_done, 1)
                v_rest(1)
                w_rest(1, q + 4)

            peeled(dve, HEADS, head)
            for j in range(2):
                y_product(HEADS - 1, j)
            y_rest(HEADS - 1)

            with dve.Fori(0, KB // 2) as i:
                for s in range(2):
                    w_rest(s, i + (Q_G_X + 1))

            def wo_rest(i, s):
                d = i * 2 + s
                dve.wait_ge(wo_hi_done[s], i + 1)
                dve.tensor_tensor(u_lo[:, d, :], side[:, s, 0:S], u_hi[:, d, :].bitcast(F32),
                                  ALU.subtract).then_inc(wo_lo_done[s], 1)

            def merge(i, s):
                d = i * 2 + s
                dve.wait_ge(gate_x_done[s], KB // 2)
                dve.wait_ge(step_done[s], i + (Q_X_OUT + 1))
                dve.tensor_tensor(merged[:, d, :], pair[s][:], merged[:, d, :], ALU.mult).then_inc(gated_x[s], 1)
                dve.wait_ge(parts_loaded[s], i * 16 + 16)
                dve.wait_ge(gated_x[s], i + 1)
                dve.tensor_tensor(merged[:, d, :], merged[:, d, :], tile[:, s, :], ALU.add).then_inc(merged_done[s], 1)

            with dve.Fori(0, KB // 2 - 1) as i:
                for s in range(2):
                    wo_rest(i, s)
                    w_rest(s, i + (Q_X_OUT + 1))
                    merge(i, s)
            def merged_rest(i, s, k=slice(0, KB), hi=hi_done, count=None, lo=lo_done):
                dve.wait_ge(hi[s], i + (Q_FINAL + 1) if count is None else count)
                dve.tensor_tensor(w_lo[:, s, :].rearrange("p (k e) -> p k e", e=P)[:, k, :],
                                  merged[:, k, bass.ds((i * 2 + s) * P, P)],
                                  w_hi[:, s, :].rearrange("p (k e) -> p k e", e=P)[:, k, :].bitcast(F32),
                                  ALU.subtract).then_inc(lo[s], 1)

            for s in range(2):
                wo_rest(KB // 2 - 1, s)
                if s == 1:
                    merged_rest(0, 0, slice(0, KB - 1), [early_hi], 1, [early_lo])
                merge(KB // 2 - 1, s)
            merged_rest(0, 0, slice(KB - 1, KB))
            merged_rest(0, 1)

            def finish(i, s):
                b = i * 2 + s
                dve.wait_ge(xres_loaded[s], i * 16 + 16)
                dve.wait_ge(step_done[s], i + (Q_FINAL + 1))
                dve.tensor_tensor(raw[:, s, :], pair[s][:], raw[:, s, :], ALU.add).then_inc(resid_done[s], 1)
                dve.wait_ge(out_root, b + 1)
                dve.reciprocal(rstd[:, bass.ds(b, 1)], rootms[:, bass.ds(b, 1)]).then_inc(out_rstd, 1)
                dve.wait_ge(out_rstd, b + 1)
                dve.wait_ge(fg_loaded, 16)
                wait(dve, out_stored[s], i * 16)
                dve.scalar_tensor_tensor(out=tile[:, s, :], in0=raw[:, s, :], scalar=rstd[:, bass.ds(b, 1)],
                                         in1=spare[:], op0=ALU.mult, op1=ALU.mult).then_inc(out_ready[s], 1)

            def finish_last():
                i, b = SB // 2 - 1, SB - 1
                dve.wait_ge(xres_loaded[1], i * 16 + 16)
                dve.wait_ge(half_done, 1)
                dve.tensor_tensor(raw[:, 1, half(0)], pair[1][:, half(0)], raw[:, 1, half(0)], ALU.add).then_inc(half_resid, 1)
                dve.wait_ge(half_sq, 1)
                dve.tensor_scalar(half_meansq, half_sumsq, 1.0 / D, EPS, ALU.mult, ALU.add).then_inc(half_mean, 1)
                dve.wait_ge(step_done[1], Q_FINAL + SB // 2)
                dve.tensor_tensor(raw[:, 1, half(1)], pair[1][:, half(1)], raw[:, 1, half(1)], ALU.add).then_inc(resid_done[1], 1)
                dve.wait_ge(out_root, b + 1)
                dve.reciprocal(rstd[:, b:b + 1], rootms[:, b:b + 1]).then_inc(out_rstd, 1)
                dve.wait_ge(out_rstd, b + 1)
                dve.wait_ge(out_stored[1], i * 16)
                for part, done in ((half(0), half_ready), (half(1), out_ready[1])):
                    dve.scalar_tensor_tensor(out=tile[:, 1, part], in0=raw[:, 1, part], scalar=rstd[:, b:b + 1],
                                             in1=spare[:, part], op0=ALU.mult, op1=ALU.mult).then_inc(done, 1)

            def finish_pair(i):
                for s in range(2):
                    merged_rest(i + 1, s)
                    finish(i, s)

            peeled(dve, SB // 2 - 1, finish_pair)
            finish(SB // 2 - 1, 0)
            finish_last()

        @block.tensor
        def _(pe):
            def block_product(slot, k, operand_hi, operand_lo, halves=(0, 1)):
                at = slice(k * P, (k + 1) * P)
                first, final = k == 0, k == KB - 1
                for weight, operand, opens, closes in ((w_hi, operand_hi, first, False),
                                                       (w_hi, operand_lo, False, False),
                                                       (w_lo, operand_hi, False, final)):
                    for b in halves:
                        last = pe.matmul(pair[slot][:, half(b)], weight[:, slot, at], operand[:, k, half(b)],
                                         start=opens, stop=closes)
                return last

            def step(slot, count, operand_hi, operand_lo):
                pe.wait_ge(lo_done[slot], count + 1)
                for k in range(KB):
                    last = block_product(slot, k, operand_hi, operand_lo)
                last.then_inc(step_done[slot], 1)

            pe.wait_ge(const_done, 2)
            pe.wait_ge(param_loaded, 16 * 8)
            for at, n in ((0, P), (P, TAPS_B * KB - P), (2 * P, PC_END - PC_CONV_A)):
                pe.transpose(pair[0][:, at:at + n], spare[0:n, at:at + P], ident[0:n, 0:n]).then_inc(param_turned, 1)
            def turn_x(g, k):
                n = g * KB + k
                if n >= 4:
                    pe.wait_ge(u_lo_done, n - 3)
                for j in range(4):
                    turned = pe.transpose(misc[:, n % 4, j * P:(j + 1) * P],
                                          glu[:, 4 * g + j, PAD_B + k * P:PAD_B + (k + 1) * P], ident[:])
                turned.then_inc(x_turned, 1)

            def half_step(slot, b):
                for k in range(KB):
                    last = block_product(slot, k, u_hi, u_lo, halves=(b,))
                if b == 1:
                    last.then_inc(step_done[slot], 1)

            pe.wait_ge(x_scaled, 4)
            ahead = 4
            for k in range(ahead):
                turn_x(0, k)
            pe.wait_ge(param_copied, 2)
            pe.wait_ge(lo_done[0], 1)
            for k in range(KB):
                pe.wait_ge(u_lo_done, k + 1)
                block_product(0, k, u_hi, u_lo, halves=(0,))
                if k + ahead < KB:
                    turn_x(0, k + ahead)
            pe.wait_ge(x_scaled, 8)
            for k in range(ahead):
                turn_x(1, k)
            pe.wait_ge(lo_done[1], 1)
            for k in range(KB):
                block_product(1, k, u_hi, u_lo, halves=(0,))
                if k + ahead < KB:
                    turn_x(1, k + ahead)
            pe.wait_ge(u_lo_done, 2 * KB)
            half_step(0, 1)
            half_step(1, 1)
            with pe.Fori(1, KB) as c:
                pe.wait_ge(gate_b_done, c)
                step(0, c + Q_B_IN, u_hi, u_lo)
                pe.wait_ge(glu_done, c)
                step(1, c + Q_B_IN, u_hi, u_lo)
            pe.wait_ge(gate_b_done, KB)

            def a_in(c):
                q = c * 2 + Q_A_IN
                wait(pe, b_a_done, c)
                step(0, q, u_hi, u_lo)
                if isinstance(c, int):
                    pe.wait_ge(glu_done, KB)
                wait(pe, z_a_done, c)
                step(1, q, u_hi, u_lo)
                pe.wait_ge(c_a_copied, c + 1)
                step(0, q + 1, u_hi, u_lo)
                pe.wait_ge(cx_done, c + 1)
                step(1, q + 1, u_hi, u_lo)

            peeled(pe, KB, a_in)

            def gate_out(branch, q, d):
                wait(pe, gate_done[branch], d)
                step(0, d + q, u_hi, u_lo)
                if isinstance(d, int) and d == 0:
                    pe.wait_ge(z_a_done if branch == "a" else z_b_done[1], KB if branch == "a" else KB // 2)
                    pe.wait_ge(y_a_lo if branch == "a" else y_b_lo, KB)
                wait(pe, gated[branch], d)
                step(1, d + q, y_hi, y_lo)

            pe.wait_ge(b_a_done, KB)
            gate_out("a", Q_A_OUT, 0)
            with pe.Fori(1, 5) as d:
                gate_out("a", Q_A_OUT, d)

            def mean_of(source, target):
                for b in range(2):
                    last = pe.matmul(target[:, half(b)], ones[:], source[:, half(b)], start=True, stop=True)
                return last

            pe.wait_ge(fills, 4)
            pe.wait_ge(ln_sum, KB - 1)
            mean_of(side[:, 0, :], misc2[:, 0, :]).then_inc(mean_done, 1)
            with pe.Fori(5, KB) as d:
                gate_out("a", Q_A_OUT, d)

            pe.wait_ge(gate_done["a"], KB)
            step(0, Q_B_Z, u_hi, u_lo)
            pe.wait_ge(ln_sqsum, KB)
            mean_of(side[:, 1, :], misc2[:, 0, :]).then_inc(var_done, 1)
            pe.wait_ge(gated["a"], KB)
            step(1, Q_B_Z, u_hi, u_lo)
            with pe.Fori(1, KB // 2) as i:
                for s in range(2):
                    pe.wait_ge(z_b_done[s], i)
                    step(s, i + Q_B_Z, u_hi, u_lo)
            pe.wait_ge(z_b_done[0], KB // 2)
            gate_out("b", Q_B_OUT, 0)
            with pe.Fori(1, 4) as d:
                gate_out("b", Q_B_OUT, d)
            pe.wait_ge(mem_scaled, MB)
            for k in range(KB):
                for b in range(MB):
                    turned = pe.transpose(score[:, k, b * P:(b + 1) * P], side[:, b, k * P:(k + 1) * P], ident[:])
            turned.then_inc(mem_turned, 1)
            with pe.Fori(4, KB) as d:
                gate_out("b", Q_B_OUT, d)

            pe.wait_ge(gate_done["b"], KB)
            pe.wait_ge(mem_lo_done, KB)

            def attend(h, j):
                if j == 0:
                    pe.wait_ge(pt_lo_done, h * MB + MB)
                    pe.wait_ge(v_lo_done, h * 2 + 2)
                cols = slice(j * P, (j + 1) * P)
                for m in range(MB):
                    for stationary, moving, first, final in ((v_hi, y_hi, m == 0, False),
                                                             (v_hi, y_lo, False, False),
                                                             (v_lo, y_hi, False, m == MB - 1)):
                        for b in range(2):
                            last = pe.matmul(misc2[:, j, half(b)], stationary[:, m, cols],
                                             moving[:, h * 2 + m, half(b)], start=first, stop=final)
                last.then_inc(pv_done, 1)

            def head(h):
                q = h * 4 + Q_ATT
                first_head = isinstance(h, int) and h == 0

                def mem_step(j):
                    pe.wait_ge(lo_done[0], q + j + 1)
                    for k in range(KB):
                        at = slice(k * P, (k + 1) * P)
                        pe.matmul(pair[0][:, 0:MEM], w_hi[:, 0, at], mem_hi[:, k, :], start=k == 0, stop=False)
                        pe.matmul(pair[0][:, 0:MEM], w_hi[:, 0, at], mem_lo[:, k, :], start=False, stop=False)
                        last = pe.matmul(pair[0][:, 0:MEM], w_lo[:, 0, at], mem_hi[:, k, :], start=False,
                                         stop=k == KB - 1)
                    last.then_inc(step_done[0], 1)

                def turn_v(j):
                    pe.wait_ge(v_copied, h * 2 + j + 1)
                    for m in range(MB):
                        turned = pe.transpose(pair[0][:, HALF + m * P:HALF + (m + 1) * P],
                                              v_turned[:, m * P:(m + 1) * P], ident[:])
                    turned.then_inc(v_turned_back, 1)

                wait(pe, v_lo_done, h * 2)
                mem_step(0)
                if first_head:
                    pe.wait_ge(gated["b"], KB)
                wait(pe, z_x_done, h * 2)
                step(1, q, u_hi, u_lo)
                pe.wait_ge(k_lo_done, h * 2 + 1)
                mem_step(1)
                if not first_head:
                    attend(h - 1, 0)
                pe.wait_ge(q_lo_done, h * 2 + 1)
                step(1, q + 1, u_hi, u_lo)
                pe.wait_ge(k_lo_done, h * 2 + 2)
                mem_step(2)
                if not first_head:
                    attend(h - 1, 1)
                pe.wait_ge(q_lo_done, h * 2 + 2)
                if not first_head:
                    pe.wait_ge(y_x_product, h * 2 - 1)
                for b in range(SB):
                    if b == SB // 2:
                        wait(pe, y_x_product, h * 2)
                    rows = slice(b * P, (b + 1) * P)
                    for j in range(2):
                        q_at = KB - 2 + j
                        pe.matmul(score[:, b, :], y_hi[:, q_at, rows], k_hi[:, j, :], start=j == 0, stop=False)
                        pe.matmul(score[:, b, :], y_hi[:, q_at, rows], k_lo[:, j, :], start=False, stop=False)
                        last = pe.matmul(score[:, b, :], y_lo[:, q_at, rows], k_hi[:, j, :], start=False, stop=j == 1)
                last.then_inc(scores_done, 1)
                turn_v(0)
                step(1, q + 2, u_hi, u_lo)
                pe.wait_ge(v_lo_done, h * 2 + 1)
                mem_step(3)
                pe.wait_ge(prob_done, h * SB + SB)
                for m in range(MB):
                    for b in range(SB):
                        turned = pe.transpose(misc2[:, m, b * P:(b + 1) * P],
                                              prob[:, b // 4, b % 4, m * P:(m + 1) * P], ident[:])
                turned.then_inc(prob_turned, 1)
                turn_v(1)
                pe.wait_ge(z_x_done, h * 2 + 1)
                step(1, q + 3, u_hi, u_lo)

            peeled(pe, HEADS, head)
            for j in range(2):
                attend(HEADS - 1, j)

            def gate_x(i):
                for s in range(2):
                    if isinstance(i, int):
                        pe.wait_ge(v_lo_done if s == 0 else z_x_done, 2 * HEADS)
                    wait(pe, gate_x_done[s], i)
                    step(s, i + Q_G_X, u_hi, u_lo)

            peeled(pe, KB // 2, gate_x)
            pe.wait_ge(y_x_lo, 2 * HEADS)

            def x_out(i):
                for s in range(2):
                    if isinstance(i, int):
                        pe.wait_ge(gate_x_done[s], KB // 2)
                    wait(pe, gated_x[s], i)
                    step(s, i + Q_X_OUT, y_hi, y_lo)

            peeled(pe, KB // 2, x_out)
            pe.wait_ge(gated_x[0], KB // 2)
            for s in range(2):
                pe.wait_ge(wo_lo_done[s], KB // 2)
            pe.wait_ge(early_lo, 1)
            for k in range(KB):
                if k == KB - 1:
                    pe.wait_ge(lo_done[0], Q_FINAL + 1)
                last = block_product(0, k, u_hi, u_lo)
            last.then_inc(step_done[0], 1)
            pe.wait_ge(gated_x[1], KB // 2)
            step(1, Q_FINAL, u_hi, u_lo)
            with pe.Fori(1, SB // 2 - 1) as i:
                for s in range(2):
                    pe.wait_ge(resid_done[s], i)
                    step(s, i + Q_FINAL, u_hi, u_lo)
            pe.wait_ge(resid_done[0], SB // 2 - 1)
            step(0, Q_FINAL + SB // 2 - 1, u_hi, u_lo)
            pe.wait_ge(resid_done[1], SB // 2 - 1)
            pe.wait_ge(lo_done[1], Q_FINAL + SB // 2)
            for b, done in ((0, half_done), (1, step_done[1])):
                for k in range(KB):
                    last = block_product(1, k, u_hi, u_lo, halves=(b,))
                last.then_inc(done, 1)


_INS = ["x", "mem", "norm_g", "w_in", "conv_a_w", "w_out_a", "conv_b_w", "conv_b_b", "ln_b_g", "ln_b_b",
        "w_out_b", "mem_norm_g", "w_kv", "w_out_x", "w_o", "final_g"]


def kernel(**inputs):
    import concourse.bacc as bacc
    from concourse.bass_utils import run_bass_kernel_spmd

    nc = bacc.Bacc("TRN2", target_bir_lowering=False, num_devices=1)
    arrays, args = {}, []
    for name in _INS:
        a = np.ascontiguousarray(inputs[name])
        arrays[f"in_{name}"] = a
        args.append(nc.dram_tensor(f"in_{name}", a.shape, mybir.dt.from_np(a.dtype), kind="ExternalInput").ap())
    args.append(nc.dram_tensor("out", (1, S, D), F32, kind="ExternalOutput").ap())
    build(nc, *args)
    result = run_bass_kernel_spmd(nc, [arrays], core_ids=[0])
    return result.results[0]["out"]
```
